# Optimizing a Trainium2 kernel written in Bass

```python
import math
import jax, jax.numpy as jnp
from jax import lax
import numpy as np

D_MODEL = 1024
BATCH = 1
SEQ = 512
DEPTH = 4

CHUNK = 64
Q_BLOCK = 128
N_MIXERS = 3
N_ATTN = (DEPTH + 2) // 3
N_RWKV = (DEPTH + 1) // 3
N_POOL = DEPTH // 3

DA_HEADS = 8
DA_HEAD_DIM = D_MODEL // DA_HEADS // 2
ROPE_THETA = 10000.0
QK_EPS = 1e-6
SUBLN_EPS = 1e-5

RW_HEAD_DIM = 64
RW_HEADS = D_MODEL // RW_HEAD_DIM
RW_DECAY_LORA = max(32, int(round(1.8 * D_MODEL ** 0.5 / 32)) * 32)
RW_AAA_LORA = max(32, int(round(1.8 * D_MODEL ** 0.5 / 32)) * 32)
RW_GATE_LORA = max(32, int(round(0.6 * D_MODEL ** 0.8 / 32)) * 32)
RW_LNX_EPS = 64e-5

POOL_WINDOWS = (2, 4, 8, 16)
POOL_GROUP = D_MODEL // len(POOL_WINDOWS)

FFN_HIDDEN = -(-8 * D_MODEL // (3 * 256)) * 256
NORM_EPS = 1e-6

kernel_name = "hybrid_diffattn_rwkv7_pool_trunk"

def rms_norm(x, g, eps=NORM_EPS):
    xf = x.astype(jnp.float32)
    y = xf * lax.rsqrt(jnp.mean(xf * xf, axis=-1, keepdims=True) + eps)
    return (y * g.astype(jnp.float32)).astype(x.dtype)

def rope_tables(T, dim):
    inv = 1.0 / (ROPE_THETA ** (jnp.arange(0, dim, 2, dtype=jnp.float32) / dim))
    ang = jnp.arange(T, dtype=jnp.float32)[:, None] * inv[None, :]
    return jnp.cos(ang), jnp.sin(ang)

def apply_rope(x, cos, sin):
    xf = x.astype(jnp.float32)
    half = xf.shape[-1] // 2
    x1, x2 = xf[..., :half], xf[..., half:]
    out = jnp.concatenate([x1 * cos - x2 * sin, x2 * cos + x1 * sin], axis=-1)
    return out.astype(x.dtype)

def diff_attention(h, w_qkv, w_o, q_gain, k_gain, lam_vec, subln_g, lambda_init):
    B, T, C = h.shape
    H, d = DA_HEADS, DA_HEAD_DIM
    qkv = h @ w_qkv
    q, k, v = jnp.split(qkv, 3, axis=-1)
    q = q.reshape(B, T, 2 * H, d).transpose(0, 2, 1, 3)
    k = k.reshape(B, T, 2 * H, d).transpose(0, 2, 1, 3)
    v = v.reshape(B, T, H, 2 * d).transpose(0, 2, 1, 3)
    q = rms_norm(q, q_gain, QK_EPS)
    k = rms_norm(k, k_gain, QK_EPS)
    cos, sin = rope_tables(T, d)
    q = apply_rope(q, cos, sin)
    k = apply_rope(k, cos, sin)

    lv = lam_vec.astype(jnp.float32)
    lam = jnp.exp(jnp.sum(lv[0] * lv[1])) - jnp.exp(jnp.sum(lv[2] * lv[3])) + lambda_init

    nb = T // Q_BLOCK
    q_blocks = q.reshape(B, 2 * H, nb, Q_BLOCK, d).transpose(2, 0, 1, 3, 4)
    k_chunk = jnp.arange(T) // CHUNK
    scale = d ** -0.5
    neg = jnp.float32(-1e30)

    def block(args):
        qb, bi = args
        s = jnp.einsum('bhqd,bhkd->bhqk', qb, k).astype(jnp.float32) * scale
        q_chunk = (bi * Q_BLOCK + jnp.arange(Q_BLOCK)) // CHUNK
        mask = k_chunk[None, :] <= q_chunk[:, None]
        s = jnp.where(mask[None, None], s, neg)
        p = jax.nn.softmax(s, axis=-1).reshape(B, H, 2, Q_BLOCK, T)
        a = p[:, :, 0] - lam * p[:, :, 1]
        return jnp.einsum('bhqk,bhkd->bhqd', a.astype(v.dtype), v)

    o = lax.map(block, (q_blocks, jnp.arange(nb)))
    o = o.transpose(1, 2, 0, 3, 4).reshape(B, H, T, 2 * d)
    o = rms_norm(o, subln_g, SUBLN_EPS) * jnp.asarray(1.0 - lambda_init, o.dtype)
    o = o.transpose(0, 2, 1, 3).reshape(B, T, C)
    return o @ w_o

def rwkv7_time_mix(h, mix, w_rkv, w_o, w0, w1, w2, a0, a1, a2, g1, g2,
                   k_k, k_a, r_k, lnx_g, lnx_b):
    B, T, C = h.shape
    H, N = RW_HEADS, RW_HEAD_DIM
    f32 = jnp.float32
    h_prev = jnp.pad(h, ((0, 0), (1, 0), (0, 0)))[:, :-1]
    dx = h_prev - h
    xr = h + dx * mix[0]
    xw = h + dx * mix[1]
    xk = h + dx * mix[2]
    xv = h + dx * mix[3]
    xa = h + dx * mix[4]
    xg = h + dx * mix[5]

    r = (xr @ w_rkv[:, :C]).astype(f32)
    k = (xk @ w_rkv[:, C:2 * C]).astype(f32)
    v = (xv @ w_rkv[:, 2 * C:]).astype(f32)
    w_log = -jax.nn.softplus(-(w0.astype(f32) + (jnp.tanh(xw @ w1) @ w2).astype(f32))) - 0.5
    decay = jnp.exp(-jnp.exp(w_log))
    a = jax.nn.sigmoid(a0.astype(f32) + ((xa @ a1) @ a2).astype(f32))
    g = (jax.nn.sigmoid(xg @ g1) @ g2).astype(f32)

    kk = (k * k_k.astype(f32)).reshape(B, T, H, N)
    kk = kk * lax.rsqrt(jnp.maximum(jnp.sum(kk * kk, axis=-1, keepdims=True), 1e-24))
    k = k * (1.0 + (a - 1.0) * k_a.astype(f32))

    def heads_t(z):
        return z.reshape(B, T, H, N).transpose(1, 0, 2, 3)

    a_h = a.reshape(B, T, H, N)
    seq_in = (heads_t(r), heads_t(decay), heads_t(k), heads_t(v),
              (-kk).transpose(1, 0, 2, 3), (kk * a_h).transpose(1, 0, 2, 3))

    def step(S, inp):
        r_t, w_t, k_t, v_t, va_t, vb_t = inp
        sa = jnp.einsum('bhij,bhj->bhi', S, va_t)
        S = S * w_t[:, :, None, :] + sa[..., None] * vb_t[:, :, None, :] + v_t[..., None] * k_t[:, :, None, :]
        y = jnp.einsum('bhij,bhj->bhi', S, r_t)
        return S, y

    S0 = jnp.zeros((B, H, N, N), f32)
    _, y = lax.scan(step, S0, seq_in)
    y = y.transpose(1, 0, 2, 3)

    mu = jnp.mean(y, axis=-1, keepdims=True)
    var = jnp.mean(jnp.square(y - mu), axis=-1, keepdims=True)
    yn = ((y - mu) * lax.rsqrt(var + RW_LNX_EPS)).reshape(B, T, C)
    yn = yn * lnx_g.astype(f32) + lnx_b.astype(f32)

    bonus = jnp.sum(r.reshape(B, T, H, N) * k.reshape(B, T, H, N) * r_k.astype(f32),
                    axis=-1, keepdims=True) * v.reshape(B, T, H, N)
    out = (yn + bonus.reshape(B, T, C)) * g
    return out.astype(h.dtype) @ w_o

def multiscale_pool(h, w_groups, scale):
    B, T, C = h.shape
    hg = h.astype(jnp.float32).reshape(B, T, len(POOL_WINDOWS), POOL_GROUP)
    outs = []
    for gi, win in enumerate(POOL_WINDOWS):
        xg = hg[:, :, gi]
        P = jnp.cumsum(jnp.pad(xg, ((0, 0), (win, 0), (0, 0))), axis=1)
        s = P[:, win:] - P[:, :T]
        cnt = jnp.minimum(jnp.arange(1, T + 1), win).astype(jnp.float32)
        outs.append(s / cnt[None, :, None] - xg)
    dpool = jnp.stack(outs, axis=2).astype(h.dtype)
    y = jnp.einsum('btgi,gio->btgo', dpool, w_groups)
    return y.reshape(B, T, C) * scale

def swiglu(h, w_in, w_out):
    gu = h @ w_in
    gate, up = jnp.split(gu, 2, axis=-1)
    return (jax.nn.silu(gate) * up) @ w_out

def setup_inputs(seed: int = 0) -> dict:
    key = jax.random.key(seed)
    ks = iter(jax.random.split(key, 40))
    C, F = D_MODEL, FFN_HIDDEN
    d = DA_HEAD_DIM
    f32 = jnp.float32

    def nrm(shape, s):
        return jax.random.normal(next(ks), shape, f32) * s

    x = nrm((BATCH, SEQ, C), 1.0)
    mix_norm = 1.0 + nrm((DEPTH, C), 0.05)
    ffn_norm = 1.0 + nrm((DEPTH, C), 0.05)
    ffn_w_in = nrm((DEPTH, C, 2 * F), C ** -0.5)
    ffn_w_out = nrm((DEPTH, F, C), F ** -0.5)

    da_wqkv = nrm((N_ATTN, C, 3 * C), C ** -0.5)
    da_wo = nrm((N_ATTN, C, C), C ** -0.5)
    da_q_gain = 1.0 + nrm((N_ATTN, d), 0.05)
    da_k_gain = 1.0 + nrm((N_ATTN, d), 0.05)
    da_lambda = nrm((N_ATTN, 4, d), 0.1)
    da_subln = 1.0 + nrm((N_ATTN, 2 * d), 0.05)

    rw_mix = jax.random.uniform(next(ks), (N_RWKV, 6, C), f32)
    rw_wrkv = nrm((N_RWKV, C, 3 * C), C ** -0.5)
    rw_wo = nrm((N_RWKV, C, C), C ** -0.5)
    ramp = -7.0 + 5.0 * (jnp.arange(C, dtype=f32) / (C - 1)) ** 0.85 + 0.5
    rw_w0 = ramp[None, :] + nrm((N_RWKV, C), 0.1)
    rw_w1 = nrm((N_RWKV, C, RW_DECAY_LORA), C ** -0.5)
    rw_w2 = nrm((N_RWKV, RW_DECAY_LORA, C), 0.1 * RW_DECAY_LORA ** -0.5)
    rw_a0 = nrm((N_RWKV, C), 0.1)
    rw_a1 = nrm((N_RWKV, C, RW_AAA_LORA), C ** -0.5)
    rw_a2 = nrm((N_RWKV, RW_AAA_LORA, C), RW_AAA_LORA ** -0.5)
    rw_g1 = nrm((N_RWKV, C, RW_GATE_LORA), C ** -0.5)
    rw_g2 = nrm((N_RWKV, RW_GATE_LORA, C), RW_GATE_LORA ** -0.5)
    rw_kk = 0.85 + nrm((N_RWKV, C), 0.05)
    rw_ka = 1.0 + nrm((N_RWKV, C), 0.05)
    rw_rk = nrm((N_RWKV, RW_HEADS, RW_HEAD_DIM), 0.1)
    rw_lnx_g = 1.0 + nrm((N_RWKV, C), 0.05)
    rw_lnx_b = nrm((N_RWKV, C), 0.01)

    pool_w = nrm((N_POOL, len(POOL_WINDOWS), POOL_GROUP, POOL_GROUP), POOL_GROUP ** -0.5)
    pool_scale = 1.0 + nrm((N_POOL, C), 0.1)

    return {
        "x": x, "mix_norm": mix_norm, "ffn_norm": ffn_norm,
        "ffn_w_in": ffn_w_in, "ffn_w_out": ffn_w_out,
        "da_wqkv": da_wqkv, "da_wo": da_wo, "da_q_gain": da_q_gain,
        "da_k_gain": da_k_gain, "da_lambda": da_lambda, "da_subln": da_subln,
        "rw_mix": rw_mix, "rw_wrkv": rw_wrkv, "rw_wo": rw_wo,
        "rw_w0": rw_w0, "rw_w1": rw_w1, "rw_w2": rw_w2,
        "rw_a0": rw_a0, "rw_a1": rw_a1, "rw_a2": rw_a2,
        "rw_g1": rw_g1, "rw_g2": rw_g2, "rw_kk": rw_kk, "rw_ka": rw_ka,
        "rw_rk": rw_rk, "rw_lnx_g": rw_lnx_g, "rw_lnx_b": rw_lnx_b,
        "pool_w": pool_w, "pool_scale": pool_scale,
    }

def reference(x, mix_norm, ffn_norm, ffn_w_in, ffn_w_out,
              da_wqkv, da_wo, da_q_gain, da_k_gain, da_lambda, da_subln,
              rw_mix, rw_wrkv, rw_wo, rw_w0, rw_w1, rw_w2, rw_a0, rw_a1, rw_a2,
              rw_g1, rw_g2, rw_kk, rw_ka, rw_rk, rw_lnx_g, rw_lnx_b,
              pool_w, pool_scale):
    ia = ir = ip = 0
    for layer in range(DEPTH):
        kind = layer % N_MIXERS
        h = rms_norm(x, mix_norm[layer])
        if kind == 0:
            lambda_init = 0.8 - 0.6 * math.exp(-0.3 * layer)
            y = diff_attention(h, da_wqkv[ia], da_wo[ia], da_q_gain[ia], da_k_gain[ia],
                               da_lambda[ia], da_subln[ia], lambda_init)
            ia += 1
        elif kind == 1:
            y = rwkv7_time_mix(h, rw_mix[ir], rw_wrkv[ir], rw_wo[ir], rw_w0[ir], rw_w1[ir], rw_w2[ir],
                               rw_a0[ir], rw_a1[ir], rw_a2[ir], rw_g1[ir], rw_g2[ir],
                               rw_kk[ir], rw_ka[ir], rw_rk[ir], rw_lnx_g[ir], rw_lnx_b[ir])
            ir += 1
        else:
            y = multiscale_pool(h, pool_w[ip], pool_scale[ip])
            ip += 1
        x = x + y
        x = x + swiglu(rms_norm(x, ffn_norm[layer]), ffn_w_in[layer], ffn_w_out[layer])
    return x


_drawn_inputs = setup_inputs


def setup_inputs(seed=0):
    import zlib

    import numpy as np

    out = dict(_drawn_inputs(seed))
    spreads = {}
    factors = {'rw_w1': 8.0, 'rw_w2': 8.0, 'rw_a0': 3.175, 'rw_lnx_b': 8.0}
    for name, (base, spread) in spreads.items():
        noise = np.random.default_rng([zlib.crc32(name.encode()), seed]).standard_normal(out[name].shape)
        drawn = base * np.exp(spread * noise) if base else spread * noise
        out[name] = __import__('jax').numpy.asarray(drawn.astype(out[name].dtype))
    for name, factor in factors.items():
        out[name] = (out[name] * factor).astype(out[name].dtype)
    return out
```

```python
import math
from contextlib import ExitStack

import numpy as np
import concourse.bass as bass
from concourse import mybir
from concourse.alu_op_type import AluOpType as ALU

F32 = mybir.dt.float32
F32R = mybir.dt.float32r
BF16 = mybir.dt.bfloat16
ACT = mybir.ActivationFunctionType
AXIS_X = mybir.AxisListType.X

P = 128
C = 1024
CT = C // P
T = 512
FH = 2816
FT = FH // P
KU = 11
HEADS = 8
D = 64
TB = T // P
RH = 16
CH = 64
NCH = T // CH
LORA = 64
GLORA = 160
NORM_EPS = 1e-6
QK_EPS = 1e-6
SUBLN_EPS = 1e-5
LNX_EPS = 64e-5
PAD = 16
WINDOWS = (2, 4, 8, 16)
EXP_SET = "natural_log_exp_and_others"
SIGMOID_SET = "sigmoid_and_others"
DECAY = math.exp(-0.5)
WARM_CORE = 2
LEVELS = 5
MIXES = ((0, CT), (2, CT), (3, CT), (1, 1), (4, 1), (5, 2))

PAR = {}
NPAR = 0
for _name, _w in (("mix_norm", 32), ("ffn_norm", 32), ("qk_gain", 32), ("subln", 2), ("rw_mix", 48),
                  ("w0", 8), ("a0", 8), ("k_k", 8), ("k_a", 8), ("r_k", 8), ("lnx_g", 8), ("lnx_b", 8),
                  ("pool_scale", 8), ("ln2_12", 1)):
    PAR[_name] = NPAR
    NPAR += _w


class Steps:

    def __init__(self, eng, sem):
        self.eng, self.sem, self.base, self.k = eng, sem, 0, 0

    def done(self, ins):
        ins.then_inc(self.sem, 1)
        self.k += 1
        self.eng.wait_ge(self.sem, self.base + self.k)

    def loop(self, start, end, per):
        base, k = self.base, self.k
        with self.eng.Fori(start, end) as i:
            self.base, self.k = i * per + (base + k - start * per), 0
            yield i
            assert self.k == per, (self.k, per)
        self.base, self.k = base, k + (end - start) * per


def plan(layers):
    stages, n = [], dict(unit=0, tile=0, sums=0, norm=0, split=0, hid=0, attn=0, v=0)

    def stage(kind, units=0, width=CT, **more):
        s = dict(kind=kind, index=len(stages), units=units, width=width, **{k + "0": v for k, v in n.items()}, **more)
        n["unit"] += units
        for key, add in {
            "sums": dict(sums=1),
            "norm": dict(norm=1, split=CT if more.get("split") else 0),
            "qkv": dict(tile=3 * CT, attn=1, v=CT),
            "core": dict(split=CT),
            "out": dict(tile=CT, sums=1),
            "up": dict(tile=2 * FT, hid=FT, norm=1, split=CT),
            "down": dict(tile=CT, sums=1),
            "windows": dict(split=CT),
            "rproj": dict(tile=3 * CT + 4, split=CT * len(MIXES), v=CT),
            "scan": dict(split=CT),
        }[kind].items():
            n[key] += add
        stages.append(s)

    stage("sums")
    for layer in layers:
        nth = layer // 3
        if layer % 3 == 0:
            stage("norm", split=True, gain=PAR["mix_norm"] + CT * layer)
            stage("qkv", units=3 * CT, src=("w_qkv", nth), nth=nth)
            stage("core", nth=nth, lam0=0.8 - 0.6 * math.exp(-0.3 * layer))
            stage("out", units=CT, src=("w_o", nth), k_tiles=CT)
        elif layer % 3 == 1:
            stage("norm", split=False, gain=PAR["mix_norm"] + CT * layer)
            stage("rproj", units=3 * CT + 4, src=("w_rwkv", nth))
            stage("scan")
            stage("out", units=CT, src=("w_ro", nth), k_tiles=CT, reload=True)
        elif layer % 3 == 2:
            stage("norm", split=False, gain=PAR["mix_norm"] + CT * layer)
            stage("windows")
            stage("out", units=CT, width=2, src=("w_pool", nth), k_tiles=2)
        stages[-1]["next_gain"] = PAR["ffn_norm"] + CT * layer
        stage("up", units=2 * FT, src=("w_up", layer))
        stage("down", units=2 * CT, width=KU, src=("w_down", layer), last=layer == layers[-1])
    return stages


def trunk(nc, A, out, layers=(0, 1, 2, 3)):
    stages = plan(layers)
    ctx = ExitStack()
    with ctx:
        base = (nc.sbuf_base + 63) // 64 * 64
        size = nc.sbuf_usable_end - base
        ctx.enter_context(nc.sbuf_tensor("arena", [P, (size - 64) // 4], F32))

        def at(name, shape, dt, offset):
            n = (int(np.prod(shape[1:])) * (2 if dt == BF16 else 4) + 63) // 64 * 64
            assert offset + n <= size - 64, (name, offset + n, size)
            return nc.alloc_sbuf_tensor_at(name, shape, dt, offset=base + offset), offset + n

        x, o = at("x", [P, CT, T], F32, 0)
        raw, o = at("raw", [P, 2, KU, P], F32, o)
        w_hi, o = at("w_hi", [P, 2, KU, P], F32R, o)
        w_lo, o = at("w_lo", [P, 2, KU, P], F32R, o)
        m_hi, o = at("m_hi", [P, CT, T], F32R, o)
        m_lo, o = at("m_lo", [P, CT, T], F32R, o)
        G = o
        hid_hi, o = at("hid_hi", [P, FT, T], F32R, o)
        hid_lo, o = at("hid_lo", [P, FT, T], F32R, o)
        hn, o = at("hn", [P, CT, PAD + T], F32, o)
        par, o = at("par", [P, NPAR], F32, o)
        ident, o = at("ident", [P, P], F32, o)
        ones, o = at("ones", [P, P], F32, o)
        pair_ones, o = at("pair_ones", [P, P], F32, o)
        tmp, o = at("tmp", [P, 6, T], F32, o)
        sq, o = at("sq", [P, 2, T], F32, o)
        acc, o = at("acc", [P, T], F32, o)
        inv_cnt, o = at("inv_cnt", [P, PAD], F32, o)
        tiny, o = at("tiny", [P, 64], F32, o)
        mask_rows, o = at("mask_rows", [1, P], BF16, o)
        mask_cols, o = at("mask_cols", [1, CH], BF16, o)
        qk, g = at("qk", [P, 2 * CT, T], F32, G)
        v_tok, g = at("v_tok", [P, TB, C], F32, g)
        cos, g = at("cos", [P, T], F32, g)
        sin, g = at("sin", [P, T], F32, g)
        prob, g = at("prob", [P, 2, 2, T], F32, g)
        mixed, g = at("mixed", [P, 2, T], F32, g)
        mixed_t, g = at("mixed_t", [P, 2, T], F32, g)
        head_o, g = at("head_o", [P, 2, P], F32, g)
        head_n, g = at("head_n", [P, 2, P], F32, g)
        lam_row, g = at("lam_row", [P, 4 * D], F32, g)
        win_a, g = at("win_a", [P, 2, PAD + T], F32, G)
        win_b, g = at("win_b", [P, 2, PAD + T], F32, g)
        pooled, g = at("pooled", [P, CT, T], F32, g)

        ar, g = at("ar", [P, 2, CT, T], F32, G)
        bk, g = at("bk", [P, 2, CT, T], F32, g)
        rv_tok, g = at("rv_tok", [P, TB, C], F32, g)
        g2, g = at("g2", [P, 2, C], F32, g)
        assert g <= G + 2 * 4 * FT * T
        second_hi, _ = at("second_hi", [P, CT, T], F32R, G)
        second_lo, _ = at("second_lo", [P, CT, T], F32R, G + 2 * 4 * CT * T)
        shift, _ = at("shift", [P, CT, T], F32, 0)
        big, _ = at("big", [P, 2, 2, CT, P], F32, 0)
        MH = G - 2 * 4 * CT * T
        HN = G + 2 * 4 * FT * T
        so_far, g = at("so_far", [P, 2, NCH, CH + 1], F32, HN)
        undo, g = at("undo", [P, 2, T], F32, g)
        kk, g = at("kk", [P, 2, T], F32, g)
        kp, g = at("kp", [P, 2, T], F32, g)
        sq_r, g = at("sq_r", [P, 2, T], F32, MH)
        rs_r, g = at("rs_r", [P, 2, T], F32, g)
        inv_x, g = at("inv_x", [P, 2, CT, CH], F32, HN)
        inv_z, g = at("inv_z", [P, 2, CT, CH], F32, g)
        half_p, g = at("half_p", [P, 2, CT, CH], F32, g)
        lower, g = at("lower", [P, 2, CT, CH], F32, g)
        ar_s, g = at("ar_s", [P, CT, 2, 2, CH], F32, MH)
        bk_s, g = at("bk_s", [P, CT, 2, 2, CH], F32, g)
        bk_t, g = at("bk_t", [P, 2, CT, P], F32, g)
        uv0, g = at("uv0", [P, C], F32, g)
        m_raw, _ = at("m_raw", [P, 2, CT, CH], F32, g)
        uv1, g = at("uv1", [P, C], F32, g)
        uv = [uv0, uv1]
        TM = HN + 4 * CT * (PAD + T) + (4 * NPAR + 63) // 64 * 64 + 3 * 4 * P
        z_g, g = at("z_g", [P, 2, T], F32, TM)
        state, g = at("state", [P, CT, P], F32, g)
        z_wa, _ = at("z_wa", [P, 2, T], F32, g - 8 * T)
        t_sb, g = at("t_sb", [P, CT, P], F32, g)
        y_tok, g = at("y_tok", [P, C], F32, g)
        w2a2, _ = at("w2a2", [P, C], F32, g - 4 * C)
        scan_masks, g = at("scan_masks", [P, 7, CH], F32, g)
        wide_mask, o = at("wide_mask", [P, P], F32, o)
        coef, o = at("coef", [P, TB, RH], F32, o)
        last_decay, o = at("last_decay", [P, CT, NCH], F32, o)

        quad = [ctx.enter_context(nc.psum_tensor(f"quad{b}", [P, 2, T], F32)) for b in range(4)]
        bank = [quad[b // 2][:, b % 2, :] for b in range(4)]
        pair = quad[2:]
        x_saved = nc.dram_tensor("x_saved", (P, CT, T), F32, kind="Internal").ap()

        def sem(name):
            return ctx.enter_context(nc.semaphore(name))

        x_loaded = [sem(f"x_loaded{k}") for k in range(CT // 2)]
        x_reloaded = sem("x_reloaded")
        const_loaded = sem("const_loaded")
        rope_loaded = sem("rope_loaded")
        raw_loaded = [sem("raw_loaded0"), sem("raw_loaded1")]
        hi_done = sem("hi_done")
        lo_done = sem("lo_done")
        unit_used = sem("unit_used")
        tile_read = [sem("tile_read0"), sem("tile_read1")]
        sq_done = sem("sq_done")
        acc_done = sem("acc_done")
        stat_done = sem("stat_done")
        rstd_done = sem("rstd_done")
        h_done = sem("h_done")
        m_hi_done = sem("m_hi_done")
        m_lo_done = sem("m_lo_done")
        silu_done = sem("silu_done")
        hid_done = sem("hid_done")
        hid_hi_done = sem("hid_hi_done")
        hid_lo_done = sem("hid_lo_done")
        act_step = sem("act_step")
        dve_step = sem("dve_step")
        setup_done = sem("setup_done")
        qk_ss = sem("qk_ss")
        qk_sq = sem("qk_sq")
        qk_rs = sem("qk_rs")
        qk_done = sem("qk_done")
        vt_done = sem("vt_done")
        v_done = sem("v_done")
        lam_sum = sem("lam_sum")
        lam_exp = sem("lam_exp")
        s_done = sem("s_done")
        max_done = sem("max_done")
        exp_done = sem("exp_done")
        mix_done = sem("mix_done")
        pt_done = sem("pt_done")
        ptc_done = sem("ptc_done")
        pv_done = sem("pv_done")
        o_done = sem("o_done")
        ors_done = sem("ors_done")
        on_done = sem("on_done")
        ot_done = sem("ot_done")
        og_done = sem("og_done")
        win_done = sem("win_done")
        out_stored = sem("out_stored")
        x_stored = sem("x_stored")
        lora_loaded = sem("lora_loaded")
        shift_done = sem("shift_done")
        blend_done = sem("blend_done")
        lora_done = sem("lora_done")
        sig_done = sem("sig_done")
        cum_done = sem("cum_done")
        decay_done = sem("decay_done")
        kk_sq = sem("kk_sq")
        kk_ss = sem("kk_ss")
        kk_cl = sem("kk_cl")
        kk_rs = sem("kk_rs")
        prod_done = sem("prod_done")
        coef_done = sem("coef_done")
        kka_done = sem("kka_done")
        tail_done = sem("tail_done")
        ar_staged = sem("ar_staged")
        bk_staged = sem("bk_staged")
        v_staged = sem("v_staged")
        big_done = sem("big_done")
        big_read = sem("big_read")
        bt_done = sem("bt_done")
        bt_read = sem("bt_read")
        mr_done = sem("mr_done")
        mr_read = sem("mr_read")
        inv_ready = sem("inv_ready")
        z_cleared = sem("z_cleared")
        small_passed = sem("small_passed")
        low_done = sem("low_done")
        p_done = sem("p_done")
        p_read = sem("p_read")
        xz_done = sem("xz_done")
        t_done = sem("t_done")
        t_read = sem("t_read")
        u_done = sem("u_done")
        u_read = sem("u_read")
        ds_done = sem("ds_done")
        s_used = sem("s_used")
        s_ready = sem("s_ready")
        y_done = sem("y_done")
        y_read = sem("y_read")
        yc_done = sem("yc_done")
        ysq_done = sem("ysq_done")
        yv_done = sem("yv_done")
        yr_done = sem("yr_done")
        yn_done = sem("yn_done")
        yt_done = sem("yt_done")
        yg_done = sem("yg_done")
        ro_done = sem("ro_done")
        gate_done = sem("gate_done")
        gated = sem("gated")

        block = ctx.enter_context(nc.Block())
        width = [w for s in stages for w in [s["width"]] * s["units"]]
        n_units = len(width)

        def ahead(s, i, units):
            u = s["unit0"] + i * units + 2
            return [width[u + k] if u + k < n_units else None for k in range(units)]

        @block.sync
        def _(sp):
            for k in range(CT // 2):
                sp.dma_start(x[:, 2 * k:2 * k + 2, :], A["x"][:, 2 * k:2 * k + 2, :]).then_inc(x_loaded[k], 16)
            for dst, src in ((par, "par"), (ident, "ident"), (pair_ones, "pair_ones"), (inv_cnt, "inv_cnt")):
                sp.dma_start(dst[:], A[src]).then_inc(const_loaded, 16)

            def load(u, src, k_tiles, slot):
                if not (isinstance(u, int) and u < 2):
                    sp.wait_ge(lo_done, u - 1)
                sp.dma_start(raw[:, slot, 0:k_tiles, :].rearrange("p k n -> p (k n)"), src
                             ).then_inc(raw_loaded[slot], 16)

            for s in stages:
                if not s["units"]:
                    continue
                src, u0 = A[s["src"][0]][s["src"][1]], s["unit0"]
                for k in range(2):
                    load(u0 + k, src[k], s["width"], k)
                if s["kind"] == "qkv":
                    if u0:
                        sp.wait_ge(unit_used, u0)
                    sp.dma_start(cos[:], A["cos"]).then_inc(rope_loaded, 16)
                    sp.dma_start(sin[:], A["sin"]).then_inc(rope_loaded, 16)
                    sp.dma_start(lam_row[:], A["lam"][s["nth"]:s["nth"] + 1, :].broadcast_to([P, 4 * D])
                                 ).then_inc(rope_loaded, 16)
                if s["kind"] == "rproj":
                    for k in range(CT // 2):
                        sp.wait_ge(x_loaded[k], 16)
                    for k in range(2):
                        sp.wait_ge(tile_read[k], s["tile0"] // 2)
                    sp.dma_start(x_saved, x[:]).then_inc(x_stored, 16)
                    sp.wait_ge(h_done, CT * s["norm0"])
                    for dst, name in ((w2a2, "w2a2"), (g2, "g2"), (scan_masks, "scan_masks"), (wide_mask, "wide_mask")):
                        sp.dma_start(dst[:], A[name]).then_inc(lora_loaded, 16)
                if s.get("reload"):
                    sp.wait_ge(y_done, 4 * NCH // 2)
                    sp.dma_start(x[:], x_saved).then_inc(x_reloaded, 16)
                with sp.Fori(1, s["units"] // 2) as i:
                    for k in range(2):
                        load(i * 2 + (u0 + k), src[i * 2 + k], s["width"], k)
            s = stages[-1]
            for j in range(CT):
                sp.wait_ge(tile_read[j % 2], (s["tile0"] + j) // 2 + 1)
                sp.dma_start(out[j], x[:, j, :]).then_inc(out_stored, 16)
            sp.wait_ge(out_stored, 16 * CT)

        @block.tensor
        def _(pe):
            def unit(u, slot, dst, hi, lo, start, stop, moving_wait=None):
                pe.wait_ge(lo_done, u + 1)
                k_tiles = len(hi)
                for k in range(k_tiles):
                    if moving_wait is not None:
                        pe.wait_ge(m_lo_done, moving_wait + k + 1)
                    nc.tensor.matmul(dst, w_hi[:, slot, k, :], hi[k], start=start and k == 0, stop=False)
                    nc.tensor.matmul(dst, w_hi[:, slot, k, :], lo[k], start=False, stop=False)
                    last = nc.tensor.matmul(dst, w_lo[:, slot, k, :], hi[k], start=False,
                                            stop=stop and k == k_tiles - 1)
                last.then_inc(unit_used, 1)

            def tile(s, i, k, moving_wait=None, hi=m_hi, lo=m_lo):
                pe.wait_ge(tile_read[k], i + s["tile0"] // 2)
                unit(i * 2 + (s["unit0"] + k), k, bank[k], [hi[:, j, :] for j in range(CT)],
                     [lo[:, j, :] for j in range(CT)], True, True, moving_wait)

            def keep_warm(free_bank, products):
                for _ in range(products):
                    nc.tensor.matmul(free_bank[:, 0:P], ones[:], ident[:], start=True, stop=True)

            pe.wait_ge(setup_done, 1)
            pe.wait_ge(const_loaded, 64)
            for s in stages:
                kind, r0 = s["kind"], s["tile0"] // 2
                if kind == "norm":
                    pe.wait_ge(acc_done, 10 * s["sums0"])
                    nc.tensor.matmul(bank[2], ones[:], acc[:], start=True, stop=True).then_inc(stat_done, 1)
                elif kind == "qkv":
                    q0, v0 = 2 * CT * s["attn0"], s["v0"]

                    def half_sums(n, slot):
                        pe.wait_ge(qk_sq, n + 1)
                        nc.tensor.matmul(bank[2 + slot], pair_ones[:], sq[:, slot, :],
                                         start=True, stop=True).then_inc(qk_ss, 1)

                    def transpose_v(n_read, slot):
                        pe.wait_ge(tile_read[slot], n_read)
                        for b in range(TB):
                            last = nc.tensor.transpose(bank[2 + slot][:, b * P:(b + 1) * P],
                                                       tmp[:, slot, b * P:(b + 1) * P], ident[:])
                        last.then_inc(vt_done, 1)

                    tile(s, 0, 0, s["split0"] - CT)
                    tile(s, 0, 1)
                    half_sums(q0, 0)
                    with pe.Fori(1, CT) as i:
                        tile(s, i, 0)
                        half_sums(i * 2 + (q0 - 1), 1)
                        tile(s, i, 1)
                        half_sums(i * 2 + q0, 0)
                    tile(s, 8, 0)
                    half_sums(q0 + 15, 1)
                    tile(s, 8, 1)
                    pe.wait_ge(qk_rs, q0 + 15)
                    transpose_v(r0 + 9, 0)
                    tile(s, 9, 0)
                    pe.wait_ge(qk_rs, q0 + 16)
                    transpose_v(r0 + 9, 1)
                    tile(s, 9, 1)
                    pe.wait_ge(v_done, v0 + 1)
                    transpose_v(r0 + 10, 0)
                    with pe.Fori(10, 12) as i:
                        tile(s, i, 0)
                        pe.wait_ge(v_done, i * 2 + (v0 - 18))
                        transpose_v(i + r0, 1)
                        tile(s, i, 1)
                        pe.wait_ge(v_done, i * 2 + (v0 - 17))
                        transpose_v(i + (r0 + 1), 0)
                    pe.wait_ge(v_done, v0 + 6)
                    transpose_v(r0 + 12, 1)
                elif kind == "core":
                    c0 = s["attn0"] - 1
                    n0 = HEADS * TB * c0

                    def scores(n):
                        h, b = divmod(n, TB)
                        if n >= 2:
                            pe.wait_ge(exp_done, n0 + n - 1)
                        nk = P * (b + 1)
                        for half in range(2):
                            r = slice(D * half, D * half + D)
                            dst = pair[n % 2][:, half, :]
                            nc.tensor.matmul(dst[:, 0:nk], qk[r, h, b * P:(b + 1) * P], qk[r, CT + h, 0:nk],
                                             start=True, stop=False)
                            last = nc.tensor.matmul(dst[:, nk - CH:nk], mask_rows[0:1, :], mask_cols[0:1, :],
                                                    start=False, stop=True)
                        last.then_inc(s_done, 1)

                    def transpose_mixed(n):
                        if n >= 1:
                            pe.wait_ge(ptc_done, n0 + n)
                        pe.wait_ge(mix_done, n0 + n + 1)
                        for j in range(n % TB + 1):
                            last = nc.tensor.transpose(bank[0][:, j * P:(j + 1) * P],
                                                       mixed[:, n % 2, j * P:(j + 1) * P], ident[:])
                        last.then_inc(pt_done, 1)

                    def times_v(n):
                        h, b = divmod(n, TB)
                        pe.wait_ge(ptc_done, n0 + n + 1)
                        if n >= 2:
                            pe.wait_ge(o_done, n0 + n - 1)
                        for j in range(b + 1):
                            last = nc.tensor.matmul(bank[1 + n % 2][:, 0:P], mixed_t[:, n % 2, j * P:(j + 1) * P],
                                                    v_tok[:, j, h * P:(h + 1) * P], start=j == 0, stop=j == b)
                        last.then_inc(pv_done, 1)

                    def transpose_o(n):
                        h, b = divmod(n, TB)
                        pe.wait_ge(on_done, n0 + n + 1)
                        if b == 0 and h >= 1:
                            pe.wait_ge(og_done, HEADS * c0 + h)
                        nc.tensor.transpose(bank[3][:, b * P:(b + 1) * P], head_n[:, n % 2, :],
                                            ident[:]).then_inc(ot_done, 1)

                    pe.wait_ge(qk_done, 2 * CT * (c0 + 1))
                    pe.wait_ge(v_done, s["v0"])
                    n_steps = HEADS * TB
                    scores(0)
                    scores(1)
                    for n in range(n_steps + 2):
                        if 1 <= n and n + 2 < n_steps:
                            pe.wait_ge(exp_done, n0 + n + 1)
                            keep_warm(pair[n % 2][:, 0, :], WARM_CORE)
                        if 1 <= n <= n_steps:
                            times_v(n - 1)
                        if n + 2 < n_steps:
                            scores(n + 2)
                        if n < n_steps:
                            transpose_mixed(n)
                        if n >= 2:
                            transpose_o(n - 2)
                elif kind == "out" and s["k_tiles"] == CT:
                    tile(s, 0, 0, s["split0"] - CT)
                    tile(s, 0, 1)
                    with pe.Fori(1, CT // 2) as i:
                        for k in range(2):
                            tile(s, i, k)
                elif kind == "out":
                    pe.wait_ge(m_lo_done, s["split0"])
                    with pe.Fori(0, CT // 2) as i:
                        for k in range(2):
                            pe.wait_ge(tile_read[k], i + r0)
                            unit(i * 2 + (s["unit0"] + k), k, bank[k], [m_hi[:, i * 2 + j, :] for j in range(2)],
                                 [m_lo[:, i * 2 + j, :] for j in range(2)], True, True)
                elif kind == "up":
                    tile(s, 0, 0, s["split0"])
                    pe.wait_ge(acc_done, 10 * s["sums0"])
                    nc.tensor.matmul(bank[2], ones[:], acc[:], start=True, stop=True).then_inc(stat_done, 1)
                    tile(s, 0, 1)
                    tile(s, 1, 0)
                    tile(s, 1, 1)
                    with pe.Fori(2, FT, 2) as i:
                        for j in range(2):
                            for k in range(2):
                                tile(s, i + j, k)
                elif kind == "down":
                    pe.wait_ge(hid_lo_done, s["hid0"])
                    with pe.Fori(0, CT // 2) as i:
                        for k in range(2):
                            pe.wait_ge(tile_read[k], i + r0)
                            for half in range(2):
                                unit(i * 4 + (s["unit0"] + 2 * k + half), half, bank[k],
                                     [hid_hi[:, half * KU + j, :] for j in range(KU)],
                                     [hid_lo[:, half * KU + j, :] for j in range(KU)], half == 0, half == 1)

                elif kind == "rproj":
                    operand = ((m_hi, m_lo), (second_hi, second_lo))

                    def transpose_rv(n, slot):
                        pe.wait_ge(tile_read[slot], n)
                        for b in range(TB):
                            last = nc.tensor.transpose(bank[2 + slot][:, b * P:(b + 1) * P],
                                                       tmp[:, slot, b * P:(b + 1) * P], ident[:])
                        last.then_inc(vt_done, 1)

                    v0 = s["v0"]
                    tile(s, 0, 0, s["split0"], *operand[0])
                    tile(s, 0, 1, None, *operand[0])
                    with pe.Fori(1, 4) as i:
                        for k in range(2):
                            tile(s, i, k, None, *operand[0])
                    pe.wait_ge(m_lo_done, s["split0"] + CT * 2)
                    with pe.Fori(4, 8) as i:
                        for k in range(2):
                            tile(s, i, k, None, *operand[1])
                    pe.wait_ge(m_lo_done, s["split0"] + 3 * CT)
                    tile(s, 8, 0, None, *operand[0])
                    tile(s, 8, 1, None, *operand[0])
                    transpose_rv(r0 + 9, 0)
                    with pe.Fori(9, 12) as i:
                        tile(s, i, 0, None, *operand[0])
                        pe.wait_ge(v_done, i * 2 + (v0 - 18))
                        transpose_rv(i + r0, 1)
                        tile(s, i, 1, None, *operand[0])
                        pe.wait_ge(v_done, i * 2 + (v0 - 17))
                        transpose_rv(i + (r0 + 1), 0)
                    pe.wait_ge(v_done, v0 + 6)
                    transpose_rv(r0 + 12, 1)
                    pe.wait_ge(m_lo_done, s["split0"] + 4 * CT)
                    tile(s, 12, 0, None, *operand[1])
                    pe.wait_ge(m_lo_done, s["split0"] + 5 * CT)
                    tile(s, 12, 1, None, *operand[0])
                    pe.wait_ge(m_lo_done, s["split0"] + 6 * CT)
                    tile(s, 13, 0, None, *operand[1])
                    tile(s, 13, 1, None, *operand[1])
                    pe.wait_ge(lora_loaded, 64)
                    pe.wait_ge(z_cleared, 1)
                    pe.wait_ge(tile_read[0], r0 + 14)
                    pe.wait_ge(tile_read[1], r0 + 14)
                    for j in range(CT):
                        if j >= 2:
                            pe.wait_ge(sig_done, 2 * (j - 1))
                        for b in range(2):
                            last = nc.tensor.matmul(quad[j % 2][:, b, :], w2a2[:, j * P:(j + 1) * P], z_wa[:, b, :],
                                                    start=True, stop=True)
                        last.then_inc(lora_done, 1)
                    pe.wait_ge(sig_done, 2 * CT)
                    def kk_sum(j):
                        pe.wait_ge(kk_sq, j + 1)
                        if j >= 2:
                            pe.wait_ge(kk_cl, j - 1)
                        nc.tensor.matmul(bank[2 + j % 2], pair_ones[:], sq_r[:, j % 2, :],
                                         start=True, stop=True).then_inc(kk_ss, 1)

                    kk_sum(0)
                    for j in range(CT):
                        if j + 1 < CT:
                            kk_sum(j + 1)
                        pe.wait_ge(prod_done, j + 1)
                        for b in range(TB):
                            last = nc.tensor.matmul(quad[2][:, 0, b * RH + 2 * j:b * RH + 2 * j + 2],
                                                    tmp[:, 3 + j % 2, b * P:(b + 1) * P], pair_ones[:, 0:P:D],
                                                    start=True, stop=True)
                        last.then_inc(coef_done, 1)
                elif kind == "scan":
                    def blocks(half):
                        for first in range(2):
                            for j in range(4 * half, 4 * half + 4):
                                for turn in range(2):
                                    c = turn ^ first
                                    yield c, turn, j

                    def wait_before_small(signal, value):
                        pe.wait_ge(signal, value)
                        pe.sem_inc(small_passed, 1)

                    def transpose_y(b, half):
                        pe.wait_ge(yn_done, b * 2 + 2)
                        for j in range(4 * half, 4 * half + 4):
                            last = nc.tensor.transpose(quad[half][:, (j % 4) // 2, T // 2 + (j % 2) * P:T // 2 + (j % 2 + 1) * P],
                                                       y_tok[:, j * P:(j + 1) * P], ident[:])
                        last.then_inc(yt_done, 1)

                    def transpose_bonus(b, half):
                        pe.wait_ge(yg_done, b * CT + (4 * half + 4))
                        for j in range(4 * half, 4 * half + 4):
                            last = nc.tensor.transpose(quad[half][:, (j % 4) // 2, T // 2 + (j % 2) * P:T // 2 + (j % 2 + 1) * P],
                                                       uv0[:, j * P:(j + 1) * P], ident[:])
                        last.then_inc(yt_done, 1)

                    def scan_pair(i, first):
                        pe.wait_ge(ar_staged, i * 4 + 4)
                        pe.wait_ge(bk_staged, i * 4 + 4)
                        for c in range(2):
                            if c:
                                pe.wait_ge(big_read, i * 4 + 2)
                                pe.wait_ge(bt_read, i * 2 + 1)
                            for j in range(CT):
                                for e in range(2):
                                    r = slice(64 * e, 64 * e + 64)
                                    last = nc.tensor.matmul(quad[e][:, j // 4, (j % 4) * P:(j % 4 + 1) * P],
                                                            bk_s[r, j, c, :, :].rearrange("p a b -> p (a b)"),
                                                            ar_s[r, j, c, :, :].rearrange("p a b -> p (a b)"),
                                                            start=True, stop=True)
                            last.then_inc(big_done, 1)
                            for j in range(CT):
                                last = nc.tensor.transpose(quad[3][:, j // 4, (j % 4) * P:(j % 4 + 1) * P],
                                                           bk_s[:, j, c, :, :].rearrange("p a b -> p (a b)"), ident[:])
                            last.then_inc(bt_done, 1)
                            if c == 0:
                                for cc in range(2):
                                    for j in range(CT):
                                        for e in range(2):
                                            r = slice(64 * e, 64 * e + 64)
                                            last = nc.tensor.matmul(
                                                quad[2][64 * cc:64 * cc + 64, e, j * CH:(j + 1) * CH],
                                                ar_s[r, j, cc, 0, :], bk_s[r, j, cc, 0, :], start=True, stop=True)
                                last.then_inc(mr_done, 1)
                        pe.wait_ge(big_read, i * 4 + 4)
                        pe.wait_ge(bt_read, i * 2 + 2)
                        pe.wait_ge(mr_read, i + 1)
                        for level in range(LEVELS):
                            pe.wait_ge(low_done, i * LEVELS + (level + 1))
                            for half in range(2):
                                wait_before_small(inv_ready, i * (1 + 2 * LEVELS) + (1 + (2 * (level - 1) + half + 1 if level else 0)))
                                if not first and level == LEVELS - 2:
                                    transpose_y(i - 1, half)
                                if not first and level == LEVELS - 1:
                                    transpose_bonus(i - 1, half)
                                for c, e, j in blocks(half):
                                    r = slice(64 * c, 64 * c + 64)
                                    last = nc.tensor.matmul(quad[half][r, e, (j % 4) * CH:(j % 4 + 1) * CH],
                                                            lower[r, e, j, :], inv_z[r, e, j, :], start=True, stop=True)
                                last.then_inc(p_done, 1)
                            for half in range(2):
                                wait_before_small(p_read, i * (2 * LEVELS) + (2 * level + half + 1))
                                for c, e, j in blocks(half):
                                    r = slice(64 * c, 64 * c + 64)
                                    cols = slice((j % 4) * CH, (j % 4 + 1) * CH)
                                    factors = (half_p, inv_x) if level < LEVELS - 1 else (inv_x, half_p)
                                    last = nc.tensor.matmul(quad[2 + half][r, e, cols],
                                                            factors[0][r, e, j, :], factors[1][r, e, j, :],
                                                            start=True, stop=True)
                                last.then_inc(xz_done, 1)
                        pe.wait_ge(inv_ready, (i + 1) * (1 + 2 * LEVELS))
                        if not first:
                            pe.wait_ge(ro_done, i * 2)
                        for c in range(2):
                            rc = slice(64 * c, 64 * c + 64)
                            n = i * 4 + 2 * c
                            pe.wait_ge(v_staged, i * 2 + (c + 1))
                            for half in range(2):
                                pe.wait_ge(s_ready, n + (half + 1))
                                for j in range(4 * half, 4 * half + 4):
                                    cols = (j % 4) * P
                                    nc.tensor.matmul(quad[3][rc, half, cols:cols + P], ar_s[:, j, c, 0, :],
                                                     state[:, j, :], start=True, stop=False)
                                    for e in range(2):
                                        last = nc.tensor.matmul(quad[3][rc, half, cols + 64 * e:cols + 64 * e + 64],
                                                                big[64:, c, e, j, 0:CH],
                                                                uv[c][64:, j * P + 64 * e:j * P + 64 * e + 64],
                                                                start=False, stop=e == 1)
                                last.then_inc(t_done, 1)
                            for half in range(2):
                                if c:
                                    pe.wait_ge(y_read, n + (half - 1))
                                nc.tensor.matmul(quad[1][rc, half, :].rearrange("p (a b) -> p a b", b=CH),
                                                 mask_rows[0:1, CH:P],
                                                 mask_cols[0:1, :].unsqueeze(1).broadcast_to([1, 8, CH]),
                                                 start=True, stop=False)
                                for j in range(4 * half, 4 * half + 4):
                                    cols = (j % 4) * P
                                    last = nc.tensor.matmul(quad[1][rc, half, cols:cols + P], ar_s[:, j, c, 1, :],
                                                            state[:, j, :], start=False, stop=False)
                                last.then_inc(s_used, 1)
                            for half in range(2):
                                wait_before_small(t_read, n + (half + 1))
                                for j in range(4 * half, 4 * half + 4):
                                    for e in range(2):
                                        cols = (j % 4) * P + 64 * e
                                        last = nc.tensor.matmul(quad[0][0:64, half, cols:cols + 64],
                                                                inv_z[rc, e, j, :], t_sb[rc, j, 64 * e:64 * e + 64],
                                                                start=True, stop=True)
                                last.then_inc(u_done, 1)
                            for half in range(2):
                                pe.wait_ge(u_read, n + (half + 1))
                                for j in range(4 * half, 4 * half + 4):
                                    cols = (j % 4) * P
                                    last = nc.tensor.matmul(quad[2][:, half, cols:cols + P], bk_t[:, c, j, :],
                                                            uv[c][:, j * P:(j + 1) * P], start=True, stop=True)
                                last.then_inc(ds_done, 1)
                            for half in range(2):
                                for j in range(4 * half, 4 * half + 4):
                                    cols = (j % 4) * P
                                    for e in range(2):
                                        last = nc.tensor.matmul(quad[1][rc, half, cols + 64 * e:cols + 64 * e + 64],
                                                                big[:, c, e, j, CH:], uv[c][:, j * P + 64 * e:j * P + 64 * e + 64],
                                                                start=False, stop=e == 1 and j % 4 == 3)
                                last.then_inc(y_done, 1)

                    scan_pair(0, True)
                    with pe.Fori(1, NCH // 2) as i:
                        scan_pair(i, False)
                    for half in range(2):
                        transpose_y(NCH // 2 - 1, half)
                    for half in range(2):
                        transpose_bonus(NCH // 2 - 1, half)
                    pe.wait_ge(ro_done, NCH)
                    for j in range(CT):
                        if j >= 2:
                            pe.wait_ge(gated, j - 1)
                        nc.tensor.matmul(bank[2 + j % 2], g2[:, 0, j * P:(j + 1) * P], z_g[:, 0, :],
                                         start=True, stop=False)
                        nc.tensor.matmul(bank[2 + j % 2], g2[0:GLORA - P, 1, j * P:(j + 1) * P], z_g[0:GLORA - P, 1, :],
                                         start=False, stop=True).then_inc(gate_done, 1)

        @block.scalar
        def _(act):
            st = Steps(act, act_step)

            def hi_ahead(s, i, units, k, k_tiles):
                if k_tiles is None:
                    return
                u = s["unit0"] + k
                act.wait_ge(unit_used, i * units + (u + 1))
                act.wait_ge(raw_loaded[k % 2], i * (8 * units) + 16 * ((u + 2) // 2 + 1))
                nc.scalar.copy(w_hi[:, k % 2, 0:k_tiles, :], raw[:, k % 2, 0:k_tiles, :]).then_inc(hi_done, 1)

            def square_tile(s, i, k):
                act.wait_ge(acc_done, i * 2 + (10 * s["sums0"] + k + 1))
                nc.scalar.activation(sq[:, k, :], x[:, i * 2 + k, :], ACT.Square).then_inc(sq_done, 1)

            act.preload_act_table_set(EXP_SET)
            act.wait_ge(setup_done, 1)
            for s in stages:
                kind, r0 = s["kind"], s["tile0"] // 2
                if kind == "sums":
                    for i in range(CT // 2):
                        act.wait_ge(x_loaded[i], 16)
                        for k in range(2):
                            square_tile(s, i, k)
                    act.wait_ge(const_loaded, 64)
                    for k in range(2):
                        act.wait_ge(raw_loaded[k], 16)
                        nc.scalar.copy(w_hi[:, k, 0:width[k], :], raw[:, k, 0:width[k], :]).then_inc(hi_done, 1)
                elif kind == "norm":
                    act.wait_ge(stat_done, s["norm0"] + 1)
                    st.done(nc.scalar.activation(tmp[:, 0, :], bank[2], ACT.Ln, bias=NORM_EPS, scale=1.0 / C))
                    nc.scalar.activation(tmp[:, 1, :], tmp[:, 0, :], ACT.Exp, scale=-0.5).then_inc(rstd_done, 1)
                    if s["split"]:
                        for k in range(CT):
                            act.wait_ge(h_done, CT * s["norm0"] + k + 1)
                            nc.scalar.copy(m_hi[:, k, :], hn[:, k, PAD:]).then_inc(m_hi_done, 1)
                elif kind == "qkv":
                    q0, v0 = 2 * CT * s["attn0"], s["v0"]

                    def take(i, k):
                        act.wait_ge(unit_used, i * 2 + (s["unit0"] + k + 1))
                        if not isinstance(i, int):
                            act.wait_ge(qk_done, i * 2 + (q0 + k - 1))
                        nc.scalar.activation(sq[:, k, :], bank[k], ACT.Square).then_inc(qk_sq, 1)
                        gain = i * 2 + (PAR["qk_gain"] + 2 * CT * s["nth"] + k)
                        nc.scalar.activation(tmp[:, k, :], bank[k], ACT.Identity,
                                             scale=par[:, bass.ds(gain, 1)]).then_inc(tile_read[k], 1)

                    def rstd(n, k):
                        act.wait_ge(qk_ss, n + 1)
                        st.done(nc.scalar.activation(tmp[:, 4 + k, :], bank[2 + k], ACT.Ln, bias=QK_EPS,
                                                     scale=1.0 / D))
                        nc.scalar.activation(tmp[:, 4 + k, :], tmp[:, 4 + k, :], ACT.Exp,
                                             scale=-0.5).then_inc(qk_rs, 1)

                    def v_take(i, k):
                        act.wait_ge(unit_used, i * 2 + (s["unit0"] + k + 1))
                        nc.scalar.copy(tmp[:, k, :], bank[k]).then_inc(tile_read[k], 1)

                    hi_ahead(s, 0, 2, 0, CT)
                    take(0, 0)
                    hi_ahead(s, 0, 2, 1, CT)
                    take(0, 1)
                    rstd(q0, 0)
                    for i in st.loop(1, CT, 2):
                        hi_ahead(s, i, 2, 0, CT)
                        take(i, 0)
                        rstd(i * 2 + (q0 - 1), 1)
                        hi_ahead(s, i, 2, 1, CT)
                        take(i, 1)
                        rstd(i * 2 + q0, 0)
                    hi_ahead(s, 8, 2, 0, CT)
                    act.wait_ge(qk_done, q0 + 15)
                    v_take(8, 0)
                    rstd(q0 + 15, 1)
                    hi_ahead(s, 8, 2, 1, CT)
                    act.wait_ge(qk_done, q0 + 16)
                    v_take(8, 1)
                    for i in st.loop(9, 12, 0):
                        for k in range(2):
                            hi_ahead(s, i, 2, k, CT)
                            act.wait_ge(vt_done, i * 2 + (v0 + k - 17))
                            v_take(i, k)
                elif kind == "core":
                    c0 = s["attn0"] - 1
                    n0, n_steps = HEADS * TB * c0, HEADS * TB
                    act.wait_ge(lam_sum, c0 + 1)
                    nc.scalar.activation(tiny[:, 2:4], tiny[:, 0:2], ACT.Exp).then_inc(lam_exp, 1)

                    def exps(n):
                        m, nk = n % 2, P * (n % TB + 1)
                        act.wait_ge(max_done, n0 + n + 1)
                        if n >= 2:
                            act.wait_ge(mix_done, n0 + n - 1)
                        for half in range(2):
                            z = 2 * m + half
                            ins = nc.scalar.activation(
                                prob[:, m, half, 0:nk], pair[m][:, half, 0:nk], ACT.Exp, scale=D ** -0.5,
                                bias=tiny[:, 8 + z:9 + z], accum_out=tiny[:, 12 + z:13 + z])
                        ins.then_inc(exp_done, 1)

                    def take_transposed(n):
                        nk = P * (n % TB + 1)
                        act.wait_ge(pt_done, n0 + n + 1)
                        if n >= 2:
                            act.wait_ge(pv_done, n0 + n - 1)
                        nc.scalar.copy(mixed_t[:, n % 2, 0:nk], bank[0][:, 0:nk]).then_inc(ptc_done, 1)

                    def o_rstd(n):
                        m = n % 2
                        act.wait_ge(o_done, n0 + n + 1)
                        st.done(nc.scalar.activation(tmp[:, 2 + m, 0:P], head_o[:, m, :], ACT.Square,
                                                     accum_out=tiny[:, 24 + m:25 + m]))
                        st.done(nc.scalar.activation(tiny[:, 26 + m:27 + m], tiny[:, 24 + m:25 + m], ACT.Ln,
                                                     bias=SUBLN_EPS, scale=1.0 / P))
                        if n >= 2:
                            act.wait_ge(on_done, n0 + n - 1)
                        nc.scalar.activation(tiny[:, 28 + m:29 + m], tiny[:, 26 + m:27 + m], ACT.Exp,
                                             scale=-0.5).then_inc(ors_done, 1)

                    exps(0)
                    for n in range(n_steps + 3):
                        if n + 1 < n_steps:
                            exps(n + 1)
                        if n < n_steps:
                            take_transposed(n)
                        if 1 <= n <= n_steps:
                            o_rstd(n - 1)
                        if n > 2 and n % TB == 2:
                            h = (n - 3) // TB
                            act.wait_ge(og_done, HEADS * c0 + h + 1)
                            nc.scalar.copy(m_hi[:, h, :], tmp[:, h % 2, :]).then_inc(m_hi_done, 1)
                elif kind in ("out", "down"):
                    per, next_norm = s["units"] // CT, s["norm0"]

                    def residual(i, k, widths, final=False):
                        for e in range(per - final):
                            hi_ahead(s, i, 2 * per, per * k + e, widths[per * k + e])
                        if final and "next_gain" in s:
                            act.wait_ge(unit_used, s["unit0"] + s["units"])
                            for j in range(CT - 1):
                                act.wait_ge(h_done, CT * next_norm + j + 1)
                                nc.scalar.copy(m_hi[:, j, :], hn[:, j, PAD:]).then_inc(m_hi_done, 1)
                        if not s.get("last"):
                            act.wait_ge(tile_read[k], i + (r0 + 1))
                            square_tile(s, i, k)
                        if final:
                            hi_ahead(s, i, 2 * per, per * k + per - 1, widths[per * k + per - 1])

                    for i in st.loop(0, CT // 2 - 1, 0):
                        for k in range(2):
                            residual(i, k, ahead(s, 0, 2 * per))
                    for k in range(2):
                        residual(CT // 2 - 1, k, ahead(s, CT // 2 - 1, 2 * per), k == 1)
                elif kind == "up":
                    act.wait_ge(h_done, CT * (s["norm0"] + 1))
                    nc.scalar.copy(m_hi[:, CT - 1, :], hn[:, CT - 1, PAD:]).then_inc(m_hi_done, 1)
                    act.wait_ge(stat_done, s["norm0"] + 1)
                    st.done(nc.scalar.activation(tmp[:, 4, :], bank[2], ACT.Ln, bias=NORM_EPS, scale=1.0 / C))
                    nc.scalar.activation(tmp[:, 5, :], tmp[:, 4, :], ACT.Exp, scale=-0.5).then_inc(rstd_done, 1)
                    act.preload_act_table(ACT.Silu)

                    def gate_up(i, widths):
                        for j in range(2):
                            hi_ahead(s, i, 4, 2 * j, widths[2 * j])
                            act.wait_ge(tile_read[0], i * 2 + (r0 + j + 1))
                            nc.scalar.activation(tmp[:, j, :], tmp[:, j, :], ACT.Silu).then_inc(silu_done, 1)
                            hi_ahead(s, i, 4, 2 * j + 1, widths[2 * j + 1])
                            act.wait_ge(hid_done, i * 2 + (s["hid0"] + j + 1))
                            nc.scalar.copy(hid_hi[:, i * 2 + j, :], tmp[:, 2 + j, :]).then_inc(hid_hi_done, 1)

                    for i in st.loop(0, FT // 2 - 1, 0):
                        gate_up(i, ahead(s, 0, 4))
                    gate_up(FT // 2 - 1, ahead(s, FT // 2 - 1, 4))
                    act.preload_act_table_set(EXP_SET)
                elif kind == "rproj":
                    v0 = s["v0"]
                    operand = (m_hi, second_hi)

                    def blend_hi(q, i, p):
                        act.wait_ge(blend_done, i * 2 + (CT * q + p + 1))
                        nc.scalar.copy(operand[q % 2][:, i * 2 + p, :], tmp[:, 4 + p, :]).then_inc(m_hi_done, 1)

                    for k in range(CT):
                        blend_hi(0, k // 2, k % 2)
                    for q, dst in ((0, ar), (1, bk)):
                        for i in st.loop(0, 4, 0):
                            for k in range(2):
                                hi_ahead(s, i + 4 * q, 2, k, CT)
                                act.wait_ge(unit_used, i * 2 + (s["unit0"] + CT * q + k + 1))
                                nc.scalar.copy(dst[:, 1, i * 2 + k, :], bank[k]).then_inc(tile_read[k], 1)
                                blend_hi(q + 1, i, k)
                    for i in st.loop(0, 4, 0):
                        for k in range(2):
                            hi_ahead(s, i + 8, 2, k, CT)
                            act.wait_ge(unit_used, i * 2 + (s["unit0"] + 2 * CT + k + 1))
                            if v0:
                                act.wait_ge(vt_done, i * 2 + (v0 + k - 1))
                            nc.scalar.copy(tmp[:, k, :], bank[k]).then_inc(tile_read[k], 1)
                            blend_hi(3, i, k)
                    act.preload_act_table_set(SIGMOID_SET)
                    for k in range(CT):
                        blend_hi(4, k // 2, k % 2)
                    hi_ahead(s, 12, 2, 0, CT)
                    act.wait_ge(vt_done, v0 + CT)
                    nc.scalar.activation(z_wa[0:LORA, 0, :], bank[0][0:LORA, :], ACT.Tanh).then_inc(tile_read[0], 1)
                    for k in range(CT):
                        blend_hi(5, k // 2, k % 2)
                    hi_ahead(s, 12, 2, 1, CT)
                    nc.scalar.copy(z_wa[LORA:, 1, :], bank[1][LORA:, :]).then_inc(tile_read[1], 1)
                    hi_ahead(s, 13, 2, 0, CT)
                    nc.scalar.activation(z_g[:, 0, :], bank[0], ACT.Sigmoid).then_inc(tile_read[0], 1)
                    hi_ahead(s, 13, 2, 1, CT)
                    nc.scalar.activation(z_g[0:GLORA - P, 1, :], bank[1][0:GLORA - P, :],
                                         ACT.Sigmoid).then_inc(tile_read[1], 1)
                    for j in range(CT):
                        act.wait_ge(lora_done, j + 1)
                        for b, (dst, name) in enumerate(((ar, "w0"), (bk, "a0"))):
                            nc.scalar.activation(dst[:, 0, j, :], quad[j % 2][:, b, :], ACT.Sigmoid,
                                                 bias=par[:, PAR[name] + j:PAR[name] + j + 1]).then_inc(sig_done, 1)
                    act.preload_act_table_set(EXP_SET)
                    def square_kk(j):
                        if j >= 2:
                            act.wait_ge(kk_ss, j - 1)
                        nc.scalar.activation(sq_r[:, j % 2, :], bk[:, 1, j, :], ACT.Square,
                                             scale=par[:, PAR["k_k"] + j:PAR["k_k"] + j + 1]).then_inc(kk_sq, 1)

                    square_kk(0)
                    for j in range(CT):
                        p = j % 2
                        act.wait_ge(cum_done, j + 1)
                        if j >= 2:
                            act.wait_ge(tail_done, j - 1)
                        chunks = ar[:, 0, j, :].rearrange("p (c t) -> p c t", t=CH)
                        nc.scalar.activation(so_far[:, p, :, 1:], chunks, ACT.Exp, scale=-DECAY)
                        nc.scalar.activation(undo[:, p, :], ar[:, 0, j, :], ACT.Exp, scale=DECAY).then_inc(decay_done, 1)
                        if j + 1 < CT:
                            square_kk(j + 1)
                        act.wait_ge(kk_cl, j + 1)
                        st.done(nc.scalar.activation(rs_r[:, p, :], rs_r[:, p, :], ACT.Ln, scale=2.0 ** 24))
                        nc.scalar.activation(rs_r[:, p, :], rs_r[:, p, :], ACT.Exp, scale=-0.5,
                                             bias=par[:, PAR["ln2_12"]:PAR["ln2_12"] + 1]).then_inc(kk_rs, 1)
                elif kind == "scan":
                    act.wait_ge(kk_rs, CT)
                    act.wait_ge(tail_done, CT)
                    def squares(b):
                        act.wait_ge(yc_done, b + 1)
                        nc.scalar.activation(t_sb[:].rearrange("p j n -> p (j n)"), y_tok[:], ACT.Square).then_inc(ysq_done, 1)

                    def deviation(b):
                        act.wait_ge(yv_done, b + 1)
                        nc.scalar.activation(tiny[:, 16:32], tiny[:, 16:32], ACT.Ln, bias=LNX_EPS,
                                             scale=1.0 / CH).then_inc(yr_done, 1)
                        act.wait_ge(yr_done, b * 2 + 1)
                        nc.scalar.activation(tiny[:, 16:32], tiny[:, 16:32], ACT.Exp, scale=-0.5).then_inc(yr_done, 1)

                    def affine(b, half):
                        act.wait_ge(yt_done, b * 4 + (half + 1))
                        for j in range(4 * half, 4 * half + 4):
                            lg, lb = PAR["lnx_g"] + j, PAR["lnx_b"] + j
                            nc.scalar.activation(ar[:, 0, j, bass.ds(b * P, P)],
                                                 quad[half][:, (j % 4) // 2, T // 2 + (j % 2) * P:T // 2 + (j % 2 + 1) * P],
                                                 ACT.Identity, scale=par[:, lg:lg + 1],
                                                 bias=par[:, lb:lb + 1]).then_inc(yg_done, 1)

                    def scan_pair(i, first):
                        for c in range(2):
                            for q in range(2):
                                nc.scalar.copy(ar_s[:, :, c, q, :],
                                               ar[:, q, :, bass.ds(i * P + c * CH, CH)]).then_inc(ar_staged, 1)
                        act.wait_ge(bt_done, i * 2 + 1)
                        nc.scalar.copy(bk_t[:, 0, :, :], quad[3][:].rearrange("p b (j n) -> p (b j) n", n=P)
                                       ).then_inc(bt_read, 1)
                        act.wait_ge(mr_done, i + 1)
                        nc.scalar.copy(m_raw[:], quad[2][:].rearrange("p e (j n) -> p e j n", n=CH)).then_inc(mr_read, 1)
                        act.wait_ge(bt_done, i * 2 + 2)
                        nc.scalar.copy(bk_t[:, 1, :, :], quad[3][:].rearrange("p b (j n) -> p (b j) n", n=P)
                                       ).then_inc(bt_read, 1)
                        for n in range(2 * LEVELS):
                            half = n % 2
                            act.wait_ge(p_done, i * (2 * LEVELS) + (n + 1))
                            if n >= 2:
                                act.wait_ge(xz_done, i * (2 * LEVELS) + (n - 1))
                            nc.scalar.copy(half_p[:, :, 4 * half:4 * half + 4, :],
                                           quad[half][:, :, 0:4 * CH].rearrange("p e (j n) -> p e j n", n=CH)
                                           ).then_inc(p_read, 1)
                            if not first and n == 1:
                                squares(i - 1)
                            if not first and n == 3:
                                deviation(i - 1)
                            if not first and n // 2 == LEVELS - 2:
                                affine(i - 1, half)
                        nc.scalar.copy(uv[0][64:, :], rv_tok[0:64, i, :]).then_inc(v_staged, 1)
                        act.wait_ge(low_done, i * LEVELS + LEVELS)
                        nc.scalar.copy(uv[1][64:, :], rv_tok[64:, i, :]).then_inc(v_staged, 1)
                        for c in range(2):
                            rc = slice(64 * c, 64 * c + 64)
                            for half in range(2):
                                act.wait_ge(t_done, i * 4 + (2 * c + half + 1))
                                nc.scalar.copy(t_sb[rc, 4 * half:4 * half + 4, :],
                                               quad[3][rc, half, :].rearrange("p (j n) -> p j n", n=P)).then_inc(t_read, 1)
                            for half in range(2):
                                act.wait_ge(y_done, i * 4 + (2 * c + half + 1))
                                nc.scalar.copy(y_tok[rc, half * T:(half + 1) * T], quad[1][rc, half, :]).then_inc(y_read, 1)

                    scan_pair(0, True)
                    with act.Fori(1, NCH // 2) as i:
                        scan_pair(i, False)
                    last_pair = NCH // 2 - 1
                    squares(last_pair)
                    deviation(last_pair)
                    affine(last_pair, 0)
                    affine(last_pair, 1)
                    for k in range(CT):
                        act.wait_ge(gated, k + 1)
                        nc.scalar.copy(m_hi[:, k, :], hn[:, k, PAD:]).then_inc(m_hi_done, 1)
                elif kind == "windows":
                    for k in range(CT):
                        act.wait_ge(win_done, k + 1)
                        nc.scalar.copy(m_hi[:, k, :], pooled[:, k, :]).then_inc(m_hi_done, 1)

        @block.gpsimd
        def _(pool):
            rwkv = [s for s in stages if s["kind"] == "rproj"]
            if not rwkv:
                return
            norm0 = rwkv[0]["norm0"]
            combine = nc.gpsimd.tensor_tensor
            pool.wait_ge(x_stored, 16)
            for k in range(CT):
                pool.wait_ge(h_done, CT * (norm0 - 1) + k + 1)
                combine(shift[:, k, :], hn[:, k, PAD - 1:PAD + T - 1], hn[:, k, PAD:], ALU.subtract).then_inc(shift_done, 1)
            for j in range(CT):
                p = j % 2
                pool.wait_ge(kka_done, j + 1)
                pool.wait_ge(decay_done, j + 1)
                combine(bk[:, 1, j, :], kp[:, p, :], undo[:, p, :], ALU.mult)
                combine(ar[:, 1, j, :].rearrange("p (c t) -> p c t", t=CH), ar[:, 1, j, :].rearrange("p (c t) -> p c t", t=CH),
                     so_far[:, p, :, 1:], ALU.mult)
                combine(bk[:, 0, j, :], kk[:, p, :], undo[:, p, :], ALU.mult).then_inc(tail_done, 1)

        @block.vector
        def _(dve):
            st = Steps(dve, dve_step)
            tt, ts, stt = nc.vector.tensor_tensor, nc.vector.tensor_scalar, nc.vector.scalar_tensor_tensor

            def lo_ahead(s, i, units, k, k_tiles):
                if k_tiles is None:
                    return
                dve.wait_ge(hi_done, i * units + (s["unit0"] + k + 3))
                tt(w_lo[:, k % 2, 0:k_tiles, :], raw[:, k % 2, 0:k_tiles, :],
                   w_hi[:, k % 2, 0:k_tiles, :].bitcast(F32), ALU.subtract).then_inc(lo_done, 1)

            def clear_sums():
                nc.vector.memset(sq[:, 1, :], 0.0).then_inc(sq_done, 1)
                nc.vector.memset(acc[:], 0.0).then_inc(acc_done, 1)

            def add_squares(s, i, k):
                dve.wait_ge(sq_done, i * 2 + (9 * s["sums0"] + k + 1))
                dve.wait_ge(acc_done, i * 2 + (10 * s["sums0"] + k + 1))
                tt(acc[:], acc[:], sq[:, (k + 1) % 2, :], ALU.add).then_inc(acc_done, 1)

            def split_lo(src, j, count):
                dve.wait_ge(m_hi_done, count + 1)
                tt(m_lo[:, j, :], src, m_hi[:, j, :].bitcast(F32), ALU.subtract).then_inc(m_lo_done, 1)

            st.done(nc.vector.memset(ones[:], 1.0))
            st.done(nc.vector.memset(mask_rows[0:1, 0:CH], -1e30))
            st.done(nc.vector.memset(mask_rows[0:1, CH:P], 0.0))
            st.done(nc.vector.memset(mask_cols[:], 1.0))
            nc.vector.memset(hn[:, :, 0:PAD], 0.0).then_inc(setup_done, 1)
            dve.wait_ge(setup_done, 1)
            for s in stages:
                kind, r0 = s["kind"], s["tile0"] // 2
                if kind == "sums":
                    clear_sums()
                    for i in st.loop(0, CT // 2, 0):
                        for k in range(2):
                            add_squares(s, i, k)
                    add_squares(s, CT // 2, 0)
                    dve.wait_ge(const_loaded, 64)
                    for k in range(2):
                        dve.wait_ge(hi_done, k + 1)
                        tt(w_lo[:, k, 0:width[k], :], raw[:, k, 0:width[k], :], w_hi[:, k, 0:width[k], :].bitcast(F32),
                           ALU.subtract).then_inc(lo_done, 1)
                elif kind == "norm":
                    dve.wait_ge(rstd_done, s["norm0"] + 1)
                    for k in range(CT + 1):
                        if k < CT:
                            stt(hn[:, k, PAD:], x[:, k, :], par[:, s["gain"] + k:s["gain"] + k + 1], tmp[:, 1, :],
                                ALU.mult, ALU.mult).then_inc(h_done, 1)
                        if k and s["split"]:
                            split_lo(hn[:, k - 1, PAD:], k - 1, s["split0"] + k - 1)
                elif kind == "qkv":
                    q0, v0 = 2 * CT * s["attn0"], s["v0"]

                    def rope(n, i, k):
                        dve.wait_ge(tile_read[k], i + (r0 + 1))
                        for a in range(0, P, D):
                            for d, e in ((0, D // 2), (D // 2, 0)):
                                st.done(nc.vector.tensor_copy(tmp[a + d:a + d + D // 2, 2 + k, :],
                                                              tmp[a + e:a + e + D // 2, k, :]))
                        st.done(tt(tmp[:, 2 + k, :], tmp[:, 2 + k, :], sin[:], ALU.mult))
                        st.done(tt(tmp[:, k, :], tmp[:, k, :], cos[:], ALU.mult))
                        st.done(tt(tmp[:, k, :], tmp[:, k, :], tmp[:, 2 + k, :], ALU.add))
                        dve.wait_ge(qk_rs, q0 + 1 + n if isinstance(n, int) else n + (q0 + 1))
                        tt(qk[:, n, :], tmp[:, k, :], tmp[:, 4 + k, :], ALU.mult).then_inc(qk_done, 1)

                    def v_put(n, k):
                        dve.wait_ge(vt_done, n + (v0 + 1))
                        nc.vector.tensor_copy(v_tok[:, :, bass.ds(n * P, P)],
                                              bank[2 + k].rearrange("p (b f) -> p b f", f=P)).then_inc(v_done, 1)

                    dve.wait_ge(rope_loaded, 48 * (s["attn0"] + 1))
                    lo_ahead(s, 0, 2, 0, CT)
                    lo_ahead(s, 0, 2, 1, CT)
                    rope(0, 0, 0)
                    for i in st.loop(1, CT, 14):
                        lo_ahead(s, i, 2, 0, CT)
                        rope(i * 2 - 1, i - 1, 1)
                        lo_ahead(s, i, 2, 1, CT)
                        rope(i * 2, i, 0)
                    lo_ahead(s, 8, 2, 0, CT)
                    rope(15, 7, 1)
                    lo_ahead(s, 8, 2, 1, CT)
                    v_put(0, 0)
                    for i in st.loop(9, 12, 0):
                        lo_ahead(s, i, 2, 0, CT)
                        v_put(i * 2 - 17, 1)
                        lo_ahead(s, i, 2, 1, CT)
                        v_put(i * 2 - 16, 0)
                    v_put(7, 1)
                elif kind == "core":
                    c0 = s["attn0"] - 1
                    n0, n_steps = HEADS * TB * c0, HEADS * TB
                    lam = lam_row[:].rearrange("p (a b d) -> p a b d", a=2, b=2)
                    st.done(tt(tmp[:, 0, 0:2 * D].rearrange("p (a d) -> p a d", a=2), lam[:, :, 0, :],
                               lam[:, :, 1, :], ALU.mult))
                    nc.vector.reduce_sum(tiny[:, 0:2], tmp[:, 0, 0:2 * D].rearrange("p (a d) -> p a d", a=2),
                                         AXIS_X).then_inc(lam_sum, 1)
                    dve.wait_ge(lam_exp, c0 + 1)
                    st.done(tt(tiny[:, 4:5], tiny[:, 3:4], tiny[:, 2:3], ALU.subtract))
                    st.done(ts(tiny[:, 4:5], tiny[:, 4:5], -s["lam0"], None, ALU.add))

                    def row_max(n):
                        m, nk = n % 2, P * (n % TB + 1)
                        dve.wait_ge(s_done, n0 + n + 1)
                        st.done(nc.vector.reduce_max(tiny[:, 16 + 2 * m:18 + 2 * m], pair[m][:, :, 0:nk], AXIS_X))
                        ts(tiny[:, 8 + 2 * m:10 + 2 * m], tiny[:, 16 + 2 * m:18 + 2 * m], -D ** -0.5, None,
                           ALU.mult).then_inc(max_done, 1)
                        dve.wait_ge(max_done, n0 + n + 1)

                    def mix(n):
                        m, nk = n % 2, P * (n % TB + 1)
                        z = 12 + 2 * m
                        dve.wait_ge(exp_done, n0 + n + 1)
                        st.done(nc.vector.reciprocal(tiny[:, 20 + 2 * m:22 + 2 * m], tiny[:, z:z + 2]))
                        st.done(stt(tiny[:, 32 + m:33 + m], tiny[:, 21 + 2 * m:22 + 2 * m], tiny[:, z:z + 1],
                                    tiny[:, 4:5], ALU.mult, ALU.mult))
                        if n >= 2:
                            dve.wait_ge(pt_done, n0 + n - 1)
                        stt(mixed[:, m, 0:nk], prob[:, m, 1, 0:nk], tiny[:, 32 + m:33 + m], prob[:, m, 0, 0:nk],
                            ALU.mult, ALU.add).then_inc(mix_done, 1)
                        dve.wait_ge(mix_done, n0 + n + 1)

                    def o_take(n):
                        m = n % 2
                        dve.wait_ge(pv_done, n0 + n + 1)
                        ts(head_o[:, m, :], bank[1 + m][:, 0:P], tiny[:, 20 + 2 * m:21 + 2 * m], None,
                           ALU.mult).then_inc(o_done, 1)
                        dve.wait_ge(o_done, n0 + n + 1)

                    def o_norm(n):
                        m = n % 2
                        dve.wait_ge(ors_done, n0 + n + 1)
                        if n >= 2:
                            dve.wait_ge(ot_done, n0 + n - 1)
                        ts(head_n[:, m, :], head_o[:, m, :], tiny[:, 28 + m:29 + m], None,
                           ALU.mult).then_inc(on_done, 1)
                        dve.wait_ge(on_done, n0 + n + 1)

                    row_max(0)
                    for n in range(n_steps + 4):
                        if n > 2 and n % TB == 2:
                            h = (n - 3) // TB
                            dve.wait_ge(ot_done, n0 + TB * (h + 1))
                            ts(tmp[:, h % 2, :], bank[3], par[:, PAR["subln"] + s["nth"]:PAR["subln"] + s["nth"] + 1],
                               1.0 - s["lam0"], ALU.mult, ALU.mult).then_inc(og_done, 1)
                            dve.wait_ge(og_done, HEADS * c0 + h + 1)
                        if n + 1 < n_steps:
                            row_max(n + 1)
                        if n < n_steps:
                            mix(n)
                        if 1 <= n <= n_steps:
                            o_take(n - 1)
                        if 2 <= n < n_steps + 2:
                            o_norm(n - 2)
                        if n > 3 and n % TB == 3:
                            h = (n - 4) // TB
                            split_lo(tmp[:, h % 2, :], h, s["split0"] + h)
                elif kind in ("out", "down"):
                    per = s["units"] // CT
                    pooling = s["src"][0] == "w_pool"

                    def residual(i, k, widths, final=False):
                        for e in range(per - 1):
                            lo_ahead(s, i, 2 * per, per * k + e, widths[per * k + e])
                        dve.wait_ge(unit_used, i * (2 * per) + (s["unit0"] + per * (k + 1)))
                        xj = x[:, i * 2 + k, :]
                        if pooling:
                            c = i * 2 + (PAR["pool_scale"] + k)
                            ins = stt(xj, bank[k], par[:, bass.ds(c, 1)], xj, ALU.mult, ALU.add)
                        else:
                            ins = tt(xj, xj, bank[k], ALU.add)
                        ins.then_inc(tile_read[k], 1)
                        if "next_gain" in s:
                            dve.wait_ge(tile_read[k], i + (r0 + 1))
                            ts(hn[:, i * 2 + k, PAD:], xj, par[:, bass.ds(i * 2 + (s["next_gain"] + k), 1)], None,
                               ALU.mult).then_inc(h_done, 1)
                        if not final:
                            lo_ahead(s, i, 2 * per, per * k + per - 1, widths[per * k + per - 1])
                        elif "next_gain" in s:
                            for j in range(CT - 1):
                                split_lo(hn[:, j, PAD:], j, s["split0"] + j)
                        if not s.get("last"):
                            add_squares(s, i, k)

                    if not s.get("last"):
                        clear_sums()
                    for i in st.loop(0, CT // 2 - 1, 0):
                        for k in range(2):
                            residual(i, k, ahead(s, 0, 2 * per))
                    widths = ahead(s, CT // 2 - 1, 2 * per)
                    for k in range(2):
                        residual(CT // 2 - 1, k, widths, k == 1)
                    if not s.get("last"):
                        add_squares(s, CT // 2, 0)
                    lo_ahead(s, CT // 2 - 1, 2 * per, 2 * per - 1, widths[2 * per - 1])
                elif kind == "up":
                    split_lo(hn[:, CT - 1, PAD:], CT - 1, s["split0"] + CT - 1)
                    rstd = tmp[:, 5, :]
                    dve.wait_ge(rstd_done, s["norm0"] + 1)

                    def gate_up(i, widths):
                        for j in range(2):
                            dve.wait_ge(unit_used, i * 4 + (s["unit0"] + 2 * j + 1))
                            tt(tmp[:, j, :], bank[0], rstd, ALU.mult).then_inc(tile_read[0], 1)
                            lo_ahead(s, i, 4, 2 * j, widths[2 * j])
                            dve.wait_ge(unit_used, i * 4 + (s["unit0"] + 2 * j + 2))
                            tt(sq[:, j, :], bank[1], rstd, ALU.mult).then_inc(tile_read[1], 1)
                            dve.wait_ge(silu_done, i * 2 + (s["hid0"] + j + 1))
                            dve.wait_ge(tile_read[1], i * 2 + (r0 + j + 1))
                            tt(tmp[:, 2 + j, :], tmp[:, j, :], sq[:, j, :], ALU.mult).then_inc(hid_done, 1)
                            dve.wait_ge(hid_done, i * 2 + (s["hid0"] + j + 1))
                            lo_ahead(s, i, 4, 2 * j + 1, widths[2 * j + 1])
                            dve.wait_ge(hid_hi_done, i * 2 + (s["hid0"] + j + 1))
                            tt(hid_lo[:, i * 2 + j, :], tmp[:, 2 + j, :], hid_hi[:, i * 2 + j, :].bitcast(F32),
                               ALU.subtract).then_inc(hid_lo_done, 1)

                    for i in st.loop(0, FT // 2 - 1, 0):
                        gate_up(i, ahead(s, 0, 4))
                    gate_up(FT // 2 - 1, ahead(s, FT // 2 - 1, 4))
                elif kind == "rproj":
                    v0, b0 = s["v0"], s["split0"]
                    operand = ((m_hi, m_lo), (second_hi, second_lo))

                    def blend(q, i, p):
                        k = i * 2 + p
                        if q == 0:
                            dve.wait_ge(shift_done, k + 1)
                        stt(tmp[:, 4 + p, :], shift[:, k, :], par[:, bass.ds(k + (PAR["rw_mix"] + CT * MIXES[q][0]), 1)],
                            hn[:, k, PAD:], ALU.mult, ALU.add).then_inc(blend_done, 1)

                    def blend_lo(q, i, p):
                        k = i * 2 + p
                        hi_t, lo_t = operand[q % 2]
                        dve.wait_ge(m_hi_done, k + (b0 + CT * q + 1))
                        tt(lo_t[:, k, :], tmp[:, 4 + p, :], hi_t[:, k, :].bitcast(F32),
                           ALU.subtract).then_inc(m_lo_done, 1)

                    def blend_all(q):
                        for k in range(CT):
                            if k >= 2:
                                blend_lo(q, (k - 2) // 2, k % 2)
                            if k >= 2 or q:
                                dve.wait_ge(m_lo_done, b0 + CT * q + max(k - 1, 0))
                            blend(q, k // 2, k % 2)
                        blend_lo(q, 3, 0)
                        blend_lo(q, 3, 1)

                    def v_put(n, k):
                        dve.wait_ge(vt_done, n + (v0 + 1))
                        nc.vector.tensor_copy(rv_tok[:, :, bass.ds(n * P, P)],
                                              bank[2 + k].rearrange("p (b f) -> p b f", f=P)).then_inc(v_done, 1)

                    dve.wait_ge(h_done, CT * s["norm0"])
                    blend_all(0)
                    for q in range(3):
                        for i in st.loop(0, 4, 0):
                            for k in range(2):
                                lo_ahead(s, i + 4 * q, 2, k, CT)
                                dve.wait_ge(unit_used, i * 2 + (s["unit0"] + CT * q + k + 1))
                                dve.wait_ge(m_lo_done, i * 2 + (b0 + CT * (q + 1) + k))
                                blend(q + 1, i, k)
                                blend_lo(q + 1, i, k)
                                if q == 2:
                                    v_put(i * 2 + k, k)
                    st.done(nc.vector.memset(z_wa[LORA:, 0, :], 0.0))
                    nc.vector.memset(z_wa[0:LORA, 1, :], 0.0).then_inc(z_cleared, 1)
                    blend_all(4)
                    lo_ahead(s, 12, 2, 0, CT)
                    dve.wait_ge(unit_used, s["unit0"] + 3 * CT + 1)
                    blend_all(5)
                    for i, k in ((12, 1), (13, 0), (13, 1)):
                        lo_ahead(s, i, 2, k, CT)
                    st.done(nc.vector.memset(so_far[:, :, :, 0:1], 1.0))
                    dve.wait_ge(lora_loaded, 64)
                    st.done(nc.vector.memset(tmp[:, 5, :], 1.0))
                    st.done(nc.vector.memset(tmp[:, 5, 0:T:CH], 0.0))

                    def col(name, j):
                        return par[:, PAR[name] + j:PAR[name] + j + 1]

                    def chunked(ap):
                        return ap.rearrange("p (c t) -> p c t", t=CH)

                    for j in range(CT + 1):
                        if j < CT:
                            p = j % 2
                            dve.wait_ge(sig_done, 2 * j + 2)
                            nc.vector.tensor_tensor_scan(ar[:, 0, j, :], tmp[:, 5, :], ar[:, 0, j, :], 0.0,
                                                         ALU.mult, ALU.add).then_inc(cum_done, 1)
                        if j == 0:
                            continue
                        j, p = j - 1, (j - 1) % 2
                        dve.wait_ge(kk_ss, j + 1)
                        ts(rs_r[:, p, :], bank[2 + p], 1e-24, None, ALU.max).then_inc(kk_cl, 1)
                        if j >= 2:
                            dve.wait_ge(tail_done, j - 1)
                        st.done(ts(kp[:, p, :], bk[:, 0, j, :], -1.0, col("k_a", j), ALU.add, ALU.mult))
                        st.done(stt(kp[:, p, :], kp[:, p, :], 1.0, bk[:, 1, j, :], ALU.add, ALU.mult))
                        if j >= 2:
                            dve.wait_ge(coef_done, j - 1)
                        stt(tmp[:, 3 + p, :], ar[:, 1, j, :], col("r_k", j), kp[:, p, :], ALU.mult,
                            ALU.mult).then_inc(prod_done, 1)
                        dve.wait_ge(prod_done, j + 1)
                        dve.wait_ge(decay_done, j + 1)
                        dve.wait_ge(kk_rs, j + 1)
                        st.done(stt(kk[:, p, :], bk[:, 1, j, :], col("k_k", j), rs_r[:, p, :], ALU.mult, ALU.mult))
                        st.done(nc.vector.tensor_copy(last_decay[:, j, :], so_far[:, p, :, CH]))
                        st.done(stt(chunked(ar[:, 0, j, :]), chunked(kk[:, p, :]), -1.0, so_far[:, p, :, 0:CH],
                                    ALU.mult, ALU.mult))
                        tt(kk[:, p, :], kk[:, p, :], bk[:, 0, j, :], ALU.mult).then_inc(kka_done, 1)
                        dve.wait_ge(kka_done, j + 1)
                    dve.wait_ge(tail_done, CT)
                    dve.wait_ge(coef_done, CT)
                    st.done(nc.vector.tensor_copy(coef[:].rearrange("p b h -> p (b h)"), quad[2][:, 0, 0:TB * RH]))
                elif kind == "scan":
                    def flat(t):
                        return t[:].rearrange("p a j c -> p (a j c)")

                    def over_heads(ap, rows=P):
                        return ap.unsqueeze(1).broadcast_to([rows, RH, CH])

                    def by_head(t):
                        return t.rearrange("p a j c -> p (a j) c")

                    nc.vector.memset(state[:], 0.0).then_inc(s_ready, 2)
                    dve.wait_ge(s_ready, 2)
                    yh = y_tok[:].rearrange("p (h n) -> p h n", n=CH)

                    def center(b):
                        dve.wait_ge(y_read, b * 4 + 4)
                        st.done(nc.vector.reduce_sum(tiny[:, 0:16], yh, AXIS_X))
                        st.done(ts(tiny[:, 0:16], tiny[:, 0:16], 1.0 / CH, None, ALU.mult))
                        tt(yh, yh, tiny[:, 0:16].unsqueeze(2).broadcast_to([P, RH, CH]), ALU.subtract).then_inc(yc_done, 1)
                        tt(uv0[:].rearrange("p (h n) -> p h n", n=CH), rv_tok[:, b, :].rearrange("p (h n) -> p h n", n=CH),
                           coef[:, b, :].unsqueeze(2).broadcast_to([P, RH, CH]), ALU.mult).then_inc(yn_done, 1)

                    def spread(b):
                        dve.wait_ge(ysq_done, b + 1)
                        nc.vector.reduce_sum(tiny[:, 16:32], t_sb[:].rearrange("p j (h n) -> p (j h) n", n=CH),
                                             AXIS_X).then_inc(yv_done, 1)

                    def scale_y(b):
                        dve.wait_ge(yr_done, b * 2 + 2)
                        tt(yh, yh, tiny[:, 16:32].unsqueeze(2).broadcast_to([P, RH, CH]), ALU.mult).then_inc(yn_done, 1)

                    def add_bonus(b, half):
                        dve.wait_ge(yt_done, b * 4 + (half + 3))
                        dve.wait_ge(yg_done, b * CT + (4 * half + 4))
                        for e in range(2):
                            y_2 = ar[:, 0, 4 * half + 2 * e:4 * half + 2 * e + 2, bass.ds(b * P, P)]
                            ins = tt(y_2, y_2, quad[half][:, e, T // 2:].rearrange("p (j n) -> p j n", n=P), ALU.add)
                            if e == 0:
                                st.done(ins)
                        ins.then_inc(ro_done, 1)
                        dve.wait_ge(ro_done, b * 2 + (half + 1))

                    def scan_pair(i, first):
                        for c in range(2):
                            for q in range(2):
                                nc.vector.tensor_copy(bk_s[:, :, c, q, :],
                                                      bk[:, q, :, bass.ds(i * P + c * CH, CH)]).then_inc(bk_staged, 1)
                        def mask_lower(level):
                            tt(by_head(lower[:]), by_head(m_raw[:]), over_heads(scan_masks[:, 1 + level, :]),
                               ALU.mult).then_inc(low_done, 1)

                        for c in range(2):
                            dve.wait_ge(big_done, i * 2 + (c + 1))
                            for e in range(2):
                                tt(big[:, c, e, :, :], quad[e][:].rearrange("p b (j n) -> p (b j) n", n=P),
                                   wide_mask[:].unsqueeze(1).broadcast_to([P, CT, P]), ALU.mult).then_inc(big_read, 1)
                            dve.wait_ge(big_read, i * 4 + (2 * c + 2))
                            if c == 0:
                                dve.wait_ge(mr_read, i + 1)
                                st.done(tt(by_head(inv_x[:]), by_head(m_raw[:]), over_heads(scan_masks[:, 0, :]), ALU.mult))
                                st.done(tt(by_head(inv_x[:]), by_head(inv_x[:]), over_heads(scan_masks[:, 6, :]), ALU.add))
                                nc.vector.transpose(flat(inv_z), flat(inv_x)).then_inc(inv_ready, 1)
                                mask_lower(0)
                        for level in range(LEVELS):
                            if level < LEVELS - 1:
                                dve.wait_ge(p_done, i * (2 * LEVELS) + (2 * level + 2))
                                mask_lower(level + 1)
                            if not first:
                                if level == 0:
                                    center(i - 1)
                                elif level == 1:
                                    spread(i - 1)
                                elif level == 2:
                                    scale_y(i - 1)
                                elif level == LEVELS - 1:
                                    for half in range(2):
                                        dve.wait_ge(p_read, i * (2 * LEVELS) + (2 * level + half + 1))
                                        add_bonus(i - 1, half)
                            for half in range(2):
                                hs = slice(4 * half, 4 * half + 4)
                                dve.wait_ge(xz_done, i * (2 * LEVELS) + (2 * level + half + 1))
                                dx = quad[2 + half][:, :, 0:4 * CH].rearrange("p e (j n) -> p e j n", n=CH)
                                if level < LEVELS - 1:
                                    st.done(tt(inv_x[:, :, hs, :], inv_x[:, :, hs, :], dx, ALU.add))
                                    nc.vector.transpose(inv_z[:, :, hs, :].rearrange("p e j n -> p e (j n)"),
                                                        inv_x[:, :, hs, :].rearrange("p e j n -> p e (j n)")
                                                        ).then_inc(inv_ready, 1)
                                else:
                                    tt(inv_z[:, :, hs, :], inv_z[:, :, hs, :], dx, ALU.add).then_inc(inv_ready, 1)
                                dve.wait_ge(inv_ready, i * (1 + 2 * LEVELS) + (2 + 2 * level + half))
                        for c in range(2):
                            n = i * 4 + 2 * c
                            for half in range(2):
                                dve.wait_ge(u_done, n + (half + 1))
                                nc.vector.tensor_copy(uv[c][0:64, half * T:(half + 1) * T],
                                                      quad[0][0:64, half, :]).then_inc(u_read, 1)
                            for half in range(2):
                                dve.wait_ge(ds_done, n + (half + 1))
                                dve.wait_ge(s_used, n + (half + 1))
                                hs = slice(4 * half, 4 * half + 4)
                                for e in range(2):
                                    r = slice(64 * e, 64 * e + 64)
                                    st.done(tt(state[r, hs, r], state[r, hs, r],
                                               quad[2][r, half, :].rearrange("p (j n) -> p j n", n=P)[:, :, r], ALU.add))
                                    decay = last_decay[r, hs, bass.ds(i * 2 + c, 1)].broadcast_to([64, 4, 64])
                                    ins = tt(state[r, hs, r], state[r, hs, r], decay, ALU.mult)
                                    if e == 0:
                                        st.done(ins)
                                ins.then_inc(s_ready, 1)
                                dve.wait_ge(s_ready, n + (half + 3))

                    scan_pair(0, True)
                    for i in st.loop(1, NCH // 2, 26):
                        scan_pair(i, False)
                    last_pair = NCH // 2 - 1
                    center(last_pair)
                    spread(last_pair)
                    scale_y(last_pair)
                    add_bonus(last_pair, 0)
                    add_bonus(last_pair, 1)
                    for k in range(CT + 1):
                        if k < CT:
                            dve.wait_ge(gate_done, k + 1)
                            tt(hn[:, k, PAD:], ar[:, 0, k, :], bank[2 + k % 2], ALU.mult).then_inc(gated, 1)
                        if k:
                            split_lo(hn[:, k - 1, PAD:], k - 1, s["split0"] + k - 1)
                    dve.wait_ge(x_reloaded, 16)
                elif kind == "windows":
                    st.done(nc.vector.memset(hn[:, :, 0:PAD], 0.0))
                    dve.wait_ge(h_done, CT * s["norm0"])
                    st.done(nc.vector.memset(win_a[:, :, 0:PAD], 0.0))
                    st.done(nc.vector.memset(win_b[:, :, 0:PAD], 0.0))
                    for g, win in enumerate(WINDOWS):
                        h2 = hn[:, 2 * g:2 * g + 2, :]
                        src, w, buf = h2, 1, 0
                        while w < win:
                            dst = (win_a, win_b)[buf][:, :, :]
                            st.done(tt(dst[:, :, PAD:], src[:, :, PAD:], src[:, :, PAD - w:PAD + T - w], ALU.add))
                            src, w, buf = dst, 2 * w, 1 - buf
                        sums, y = src[:, :, PAD:], pooled[:, 2 * g:2 * g + 2, :]
                        for j in range(2):
                            st.done(tt(y[:, j, 0:win], sums[:, j, 0:win], inv_cnt[:, 0:win], ALU.mult))
                        st.done(tt(y[:, :, 0:win], y[:, :, 0:win], h2[:, :, PAD:PAD + win], ALU.subtract))
                        for j in range(2):
                            stt(y[:, j, win:], sums[:, j, win:], 1.0 / win, h2[:, j, PAD + win:], ALU.mult,
                                ALU.subtract).then_inc(win_done, 1)
                            dve.wait_ge(win_done, 2 * g + j + 1)
                    for k in range(CT):
                        split_lo(pooled[:, k, :], k, s["split0"] + k)


def constants():
    half = D // 2
    inv = np.float32(1.0) / (np.float32(10000.0) ** (np.arange(0, D, 2, dtype=np.float32) / np.float32(D)))
    ang = np.arange(T, dtype=np.float32)[:, None] * inv[None, :].astype(np.float32)
    cos, sin = np.cos(ang).T.astype(np.float32), np.sin(ang).T.astype(np.float32)
    eye2 = np.kron(np.eye(2, dtype=np.float32), np.ones((D, D), np.float32))
    row, column = np.arange(CH)[:, None], np.arange(CH)[None, :]
    joins = [(row // (2 * b) == column // (2 * b)) & (row // b > column // b) for b in (1, 2, 4, 8, 16, 32)]
    masks = np.stack([*joins, row == column], axis=1).astype(np.float32)
    masks = np.concatenate([masks, masks])
    wide = np.tile(np.concatenate([row < column, row <= column], axis=1), (2, 1)).astype(np.float32)
    return {
        "cos": np.tile(cos, (P // half, 1)),
        "sin": np.tile(np.concatenate([-sin, sin]), (P // D, 1)),
        "ident": np.eye(P, dtype=np.float32),
        "pair_ones": eye2,
        "scan_masks": masks, "wide_mask": wide,
        "inv_cnt": np.tile(np.float32(1.0) / np.arange(1, PAD + 1, dtype=np.float32), (P, 1)),
    }


def units_of(w):
    k, n = w.shape
    return np.ascontiguousarray(w.reshape(k // P, P, n // P, P).transpose(2, 1, 0, 3)).reshape(n // P, P, -1)


def layout(i):
    tiles = lambda v: v.reshape(-1, P).T
    par = np.zeros((P, NPAR), np.float32)

    def put(name, cols):
        par[:, PAR[name]:PAR[name] + cols.shape[1]] = cols
    for name in ("mix_norm", "ffn_norm", "rw_mix", "pool_scale"):
        put(name, tiles(i[name]))
    for name, key in (("w0", "rw_w0"), ("a0", "rw_a0"), ("k_k", "rw_kk"), ("k_a", "rw_ka"), ("r_k", "rw_rk")):
        put(name, tiles(i[key]))
    put("subln", tiles(i["da_subln"]))
    put("lnx_g", tiles(i["rw_lnx_g"]))
    put("lnx_b", tiles(i["rw_lnx_b"]))
    par[:, PAR["ln2_12"]] = 12 * math.log(2)
    gains = [np.tile(np.tile(g[n], P // D)[:, None], (1, CT)) for n in range(2)
             for g in (i["da_q_gain"], i["da_k_gain"])]
    put("qk_gain", np.concatenate(gains, axis=1))
    up = []
    for w in i["ffn_w_in"]:
        u = units_of(w)
        up.append(np.stack([u[:FT], u[FT:]], axis=1).reshape(2 * FT, P, -1))
    down = [w.reshape(2, KU, P, CT, P).transpose(3, 0, 2, 1, 4).reshape(2 * CT, P, KU * P) for w in i["ffn_w_out"]]
    def padded(w, before, width):
        out = np.zeros((C, width), np.float32)
        out[:, before:before + w.shape[1]] = w
        return out

    g2 = np.zeros((2 * P, C), np.float32)
    g2[:GLORA] = i["rw_g2"][0]
    rwkv = np.concatenate([i["rw_wrkv"][0], padded(i["rw_w1"][0], 0, P), padded(i["rw_a1"][0], LORA, P),
                           padded(i["rw_g1"][0], 0, 2 * P)], axis=1)
    return {
        "w_rwkv": units_of(rwkv)[None],
        "w_ro": units_of(i["rw_wo"][0])[None],
        "w2a2": np.concatenate([i["rw_w2"][0], i["rw_a2"][0]]),
        "g2": np.ascontiguousarray(g2.reshape(2, P, C).transpose(1, 0, 2)),
        "x": np.ascontiguousarray(i["x"][0].T.reshape(CT, P, T).transpose(1, 0, 2)),
        "par": par,
        "lam": np.ascontiguousarray(i["da_lambda"].reshape(2, -1)),
        "w_qkv": np.stack([units_of(w) for w in i["da_wqkv"]]),
        "w_o": np.stack([units_of(w) for w in i["da_wo"]]),
        "w_up": np.stack(up),
        "w_down": np.ascontiguousarray(np.stack(down)),
        "w_pool": np.stack([np.concatenate([units_of(w) for w in ws]) for ws in i["pool_w"]]),
        **constants(),
    }


def kernel(**inputs):
    import concourse.bacc as bacc
    from concourse.bass_utils import run_bass_kernel_spmd

    arrays = layout({k: np.asarray(v) for k, v in inputs.items()})
    nc = bacc.Bacc("TRN2", target_bir_lowering=False, num_devices=1)
    A = {n: nc.dram_tensor(n, a.shape, mybir.dt.from_np(a.dtype), kind="ExternalInput").ap() for n, a in arrays.items()}
    out = nc.dram_tensor("out", (CT, P, T), F32, kind="ExternalOutput").ap()
    trunk(nc, A, out)
    got = run_bass_kernel_spmd(nc, [arrays], core_ids=[0]).results[0]["out"]
    return np.ascontiguousarray(got.reshape(C, T).T)[None]
```
